# Optimizing a Trainium2 kernel written in Bass

```python
import jax, jax.numpy as jnp
from jax import lax
import numpy as np

D_MODEL = 1024
BATCH = 1
SEQ = 1024
DEPTH = 1
DEC_BATCH = 8
DEC_SEQ = 4
PAST_LEN = 2048
PAGE_SIZE = 128

PLE_DIM = 256
POOL_WIDTH = D_MODEL
POOL_WINDOWS = (2, 4, 8, 16)
N_POOL_GROUPS = len(POOL_WINDOWS)
POOL_GROUP = POOL_WIDTH // N_POOL_GROUPS
POOL_STATE = max(POOL_WINDOWS) - 1
HEAD_DIM = 64
N_HEADS = D_MODEL // HEAD_DIM
N_KV_HEADS = 4
GQA_GROUP = N_HEADS // N_KV_HEADS
ATTN_WIDTH = N_HEADS * HEAD_DIM
KV_WIDTH = N_KV_HEADS * HEAD_DIM
WINDOW = 128
BLOCK = 128
ROPE_THETA = 500000.0
ROPE_DIM = HEAD_DIM // 4
EPS = 1e-6
IN_SPLIT_SIZES = (POOL_WIDTH, POOL_WIDTH, ATTN_WIDTH, KV_WIDTH, KV_WIDTH, ATTN_WIDTH, D_MODEL, D_MODEL)
IN_COLS = sum(IN_SPLIT_SIZES)
IN_SPLIT_POINTS = tuple(int(c) for c in np.cumsum(IN_SPLIT_SIZES)[:-1])

kernel_name = "hybrid_pool_swa_gated_decoder_step"

def rms_norm(x, g):
    xf = x.astype(jnp.float32)
    y = xf * lax.rsqrt(jnp.mean(xf * xf, axis=-1, keepdims=True) + EPS) * g.astype(jnp.float32)
    return y.astype(x.dtype)

def rope(x, pos):
    inv_freq = ROPE_THETA ** (-jnp.arange(0, ROPE_DIM, 2, dtype=jnp.float32) / ROPE_DIM)
    ang = pos.astype(jnp.float32)[:, None] * inv_freq[None, :]
    cos = jnp.cos(ang)[None, :, None, :]
    sin = jnp.sin(ang)[None, :, None, :]
    xr = x[..., :ROPE_DIM].astype(jnp.float32)
    x1, x2 = xr[..., :ROPE_DIM // 2], xr[..., ROPE_DIM // 2:]
    rot = jnp.concatenate([x1 * cos - x2 * sin, x2 * cos + x1 * sin], axis=-1).astype(x.dtype)
    return jnp.concatenate([rot, x[..., ROPE_DIM:]], axis=-1)

def multiscale_pool(u_pad, pos, pool_map, pool_scale):
    B, L, P = u_pad.shape
    T = L - POOL_STATE
    uf = u_pad.astype(jnp.float32)
    cs = jnp.concatenate([jnp.zeros_like(uf[:, :1]), jnp.cumsum(uf, axis=1)], axis=1)
    end = cs[:, POOL_STATE + 1:]
    u = uf[:, POOL_STATE:]
    outs = []
    for g, w in enumerate(POOL_WINDOWS):
        sl = slice(g * POOL_GROUP, (g + 1) * POOL_GROUP)
        start = cs[:, POOL_STATE + 1 - w: POOL_STATE + 1 - w + T, sl]
        cnt = jnp.minimum(pos + 1, w).astype(jnp.float32)[None, :, None]
        outs.append((end[..., sl] - start) / cnt - u[..., sl])
    r = jnp.stack(outs, axis=2)
    r = jnp.einsum('btgc,gcd->btgd', r, pool_map.astype(jnp.float32)).reshape(B, T, P)
    return (r * pool_scale.astype(jnp.float32)).astype(u_pad.dtype)

def sw_attention_core(q, k, v, qpos, kpos, sinks):
    s = jnp.einsum('bnqkgd,bnskd->bnkgqs', q.astype(jnp.float32), k.astype(jnp.float32)) * (HEAD_DIM ** -0.5)
    rel = qpos[:, :, None] - kpos[:, None, :]
    mask = (rel >= 0) & (rel <= WINDOW) & (kpos[:, None, :] >= 0)
    s = jnp.where(mask[None, :, None, None], s, -jnp.inf)
    sink = sinks.astype(jnp.float32).reshape(N_KV_HEADS, GQA_GROUP)[None, None, :, :, None, None]
    m = jnp.maximum(jnp.max(s, axis=-1, keepdims=True), sink)
    e = jnp.exp(s - m)
    pr = e / (jnp.sum(e, axis=-1, keepdims=True) + jnp.exp(sink - m))
    return jnp.einsum('bnkgqs,bnskd->bnqkgd', pr, v.astype(jnp.float32))

def layer(h, p_l, pos, pool_prev, k_prev, v_prev, norm_g, w_in, q_norm_g, k_norm_g, sinks,
          pool_map, pool_scale, w_proj_pool, w_proj_attn, w_out, w_ple, w_ple_gate):
    B, T, _ = h.shape
    xn = rms_norm(h, norm_g)
    z = xn @ w_in
    u, zp, q, k, v, za, ga, gb = jnp.split(z, IN_SPLIT_POINTS, axis=-1)
    if pool_prev is None:
        pool_prev = jnp.zeros((B, POOL_STATE, POOL_WIDTH), u.dtype)
    u_pad = jnp.concatenate([pool_prev, u], axis=1)
    ya = multiscale_pool(u_pad, pos, pool_map, pool_scale) * jax.nn.silu(zp)
    new_pool = u_pad[:, -POOL_STATE:]
    q = rope(rms_norm(q.reshape(B, T, N_HEADS, HEAD_DIM), q_norm_g), pos)
    k = rope(rms_norm(k.reshape(B, T, N_KV_HEADS, HEAD_DIM), k_norm_g), pos)
    v = v.reshape(B, T, N_KV_HEADS, HEAD_DIM)
    if k_prev is None:
        nb = T // BLOCK
        qb = q.reshape(B, nb, BLOCK, N_KV_HEADS, GQA_GROUP, HEAD_DIM)
        kb = k.reshape(B, nb, BLOCK, N_KV_HEADS, HEAD_DIM)
        vb = v.reshape(B, nb, BLOCK, N_KV_HEADS, HEAD_DIM)
        kcat = jnp.concatenate([jnp.concatenate([jnp.zeros_like(kb[:, :1]), kb[:, :-1]], axis=1), kb], axis=2)
        vcat = jnp.concatenate([jnp.concatenate([jnp.zeros_like(vb[:, :1]), vb[:, :-1]], axis=1), vb], axis=2)
        qpos = pos.reshape(nb, BLOCK)
        kpos = jnp.concatenate([qpos - BLOCK, qpos], axis=1)
        o = sw_attention_core(qb, kcat, vcat, qpos, kpos, sinks)
        new_k, new_v = k[:, -WINDOW:], v[:, -WINDOW:]
    else:
        kc = jnp.concatenate([k_prev, k], axis=1)
        vc = jnp.concatenate([v_prev, v], axis=1)
        kpos = jnp.concatenate([pos[0] - WINDOW + jnp.arange(WINDOW, dtype=jnp.int32), pos])[None]
        qb = q.reshape(B, 1, T, N_KV_HEADS, GQA_GROUP, HEAD_DIM)
        o = sw_attention_core(qb, kc[:, None], vc[:, None], pos[None], kpos, sinks)
        new_k, new_v = kc[:, -WINDOW:], vc[:, -WINDOW:]
    yb = o.reshape(B, T, ATTN_WIDTH).astype(h.dtype) * jax.nn.silu(za)
    m = jax.nn.sigmoid(ga) * (ya @ w_proj_pool) + jax.nn.sigmoid(gb) * (yb @ w_proj_attn)
    h = h + m @ w_out
    h = h + jax.nn.sigmoid(h @ w_ple_gate) * (p_l @ w_ple)
    return h, new_pool, new_k, new_v

def setup_inputs(seed: int = 0) -> dict:
    key = jax.random.key(seed)
    ks = jax.random.split(key, 20)
    f32 = jnp.float32
    nrm = lambda k, s, sc: jax.random.normal(k, s, f32) * sc
    return {
        "x_prompt": nrm(ks[0], (BATCH, SEQ, D_MODEL), 1.0),
        "x_sample": nrm(ks[1], (DEC_BATCH, DEC_SEQ, D_MODEL), 1.0),
        "cache_k": nrm(ks[2], (DEPTH, DEC_BATCH, WINDOW, N_KV_HEADS, HEAD_DIM), 1.0),
        "cache_v": nrm(ks[3], (DEPTH, DEC_BATCH, WINDOW, N_KV_HEADS, HEAD_DIM), 1.0),
        "state_pool": nrm(ks[4], (DEPTH, DEC_BATCH, POOL_STATE, POOL_WIDTH), 1.0),
        "p_prompt": nrm(ks[5], (DEPTH, BATCH, SEQ, PLE_DIM), 1.0),
        "p_sample": nrm(ks[6], (DEPTH, DEC_BATCH, DEC_SEQ, PLE_DIM), 1.0),
        "norm_g": 1.0 + nrm(ks[7], (DEPTH, D_MODEL), 0.05),
        "w_in": nrm(ks[8], (DEPTH, D_MODEL, IN_COLS), D_MODEL ** -0.5),
        "q_norm_g": 1.0 + nrm(ks[9], (DEPTH, HEAD_DIM), 0.05),
        "k_norm_g": 1.0 + nrm(ks[10], (DEPTH, HEAD_DIM), 0.05),
        "sinks": nrm(ks[11], (DEPTH, N_HEADS), 0.5),
        "pool_map": nrm(ks[12], (DEPTH, N_POOL_GROUPS, POOL_GROUP, POOL_GROUP), POOL_GROUP ** -0.5),
        "pool_scale": 1.0 + nrm(ks[13], (DEPTH, POOL_WIDTH), 0.1),
        "w_proj_pool": nrm(ks[14], (DEPTH, POOL_WIDTH, D_MODEL), POOL_WIDTH ** -0.5),
        "w_proj_attn": nrm(ks[15], (DEPTH, ATTN_WIDTH, D_MODEL), ATTN_WIDTH ** -0.5),
        "w_out": nrm(ks[16], (DEPTH, D_MODEL, D_MODEL), D_MODEL ** -0.5),
        "w_ple": nrm(ks[17], (DEPTH, PLE_DIM, D_MODEL), PLE_DIM ** -0.5),
        "w_ple_gate": nrm(ks[18], (DEPTH, D_MODEL, D_MODEL), D_MODEL ** -0.5),
    }

def reference(x_prompt, x_sample, cache_k, cache_v, state_pool, p_prompt, p_sample,
              norm_g, w_in, q_norm_g, k_norm_g, sinks, pool_map, pool_scale,
              w_proj_pool, w_proj_attn, w_out, w_ple, w_ple_gate):
    pos_prompt = jnp.arange(SEQ, dtype=jnp.int32)
    pos_sample = PAST_LEN + jnp.arange(DEC_SEQ, dtype=jnp.int32)
    hp, hs = x_prompt, x_sample
    kp_l, vp_l, pp_l, ks_l, vs_l, ps_l = [], [], [], [], [], []
    for i in range(DEPTH):
        w = (norm_g[i], w_in[i], q_norm_g[i], k_norm_g[i], sinks[i], pool_map[i], pool_scale[i],
             w_proj_pool[i], w_proj_attn[i], w_out[i], w_ple[i], w_ple_gate[i])
        hp, npool, nk, nv = layer(hp, p_prompt[i], pos_prompt, None, None, None, *w)
        pp_l.append(npool); kp_l.append(nk); vp_l.append(nv)
        hs, npool, nk, nv = layer(hs, p_sample[i], pos_sample, state_pool[i], cache_k[i], cache_v[i], *w)
        ps_l.append(npool); ks_l.append(nk); vs_l.append(nv)
    new_k_prompt = jnp.stack(kp_l, axis=0)
    new_v_prompt = jnp.stack(vp_l, axis=0)
    new_pool_prompt = jnp.stack(pp_l, axis=0)
    new_k_sample = jnp.stack(ks_l, axis=0)
    new_v_sample = jnp.stack(vs_l, axis=0)
    new_pool_sample = jnp.stack(ps_l, axis=0)
    return (hp, hs, new_k_prompt, new_v_prompt, new_pool_prompt, new_k_sample, new_v_sample, new_pool_sample)


_drawn_inputs = setup_inputs


def setup_inputs(seed=0):
    import zlib

    import numpy as np

    out = dict(_drawn_inputs(seed))
    spreads = {}
    factors = {'q_norm_g': 8.0, 'sinks': 64.0}
    for name, (base, spread) in spreads.items():
        noise = np.random.default_rng([zlib.crc32(name.encode()), seed]).standard_normal(out[name].shape)
        drawn = base * np.exp(spread * noise) if base else spread * noise
        out[name] = __import__('jax').numpy.asarray(drawn.astype(out[name].dtype))
    for name, factor in factors.items():
        out[name] = (out[name] * factor).astype(out[name].dtype)
    return out
```

```python
from contextlib import ExitStack

import numpy as np

import concourse.bass as bass
from concourse import mybir

F32 = mybir.dt.float32
F32R = mybir.dt.float32r
ALU = mybir.AluOpType
ACT = mybir.ActivationFunctionType
AX_X = mybir.AxisListType.X

P = 128
D = 1024
KT = D // P
SEQ, NB, NT = 1024, 8, 4
NS = NB * NT
T = SEQ + NS
NCH = 3
CH = T // NCH
PBLK = SEQ // P
HD, NH, NKV, G = 64, 16, 4, 4
HIST = 15
SEG = HIST + NT
UL = HIST + SEQ + NB * SEG
PLE = 256
EPS = 1e-6
NEG = -3.0e38
WC = 256
XKT = 2
SEQ_ORDER = (0, 2, 4, 6, 1, 3, 5, 7)
COL = dict(u=0, zp=D, q=2 * D, k=3 * D, v=3 * D + 256, za=3 * D + 512, ga=4 * D + 512, gb=5 * D + 512)

X_TILE = 2
QKV_TILE = X_TILE + KT
GATE_TILE = QKV_TILE + 12
POOL_TILE = GATE_TILE + 24
PP_TILE = POOL_TILE + 24
PA_TILE = PP_TILE + 8
WO_TILE = PA_TILE + 8
FIN_TILE = WO_TILE + 8
QKV_CHUNK, GATE_CHUNK, POOL_CHUNK, PP_CHUNK, PA_CHUNK, WO_CHUNK, FIN_CHUNK = 0, 6, 18, 26, 30, 34, 38


def chunk_end(n):
    if n < GATE_CHUNK:
        return QKV_TILE + 2 * (n + 1)
    if n < POOL_CHUNK:
        return GATE_TILE + 2 * (n - GATE_CHUNK + 1)
    if n < PP_CHUNK:
        g, second = divmod(n - POOL_CHUNK, 2)
        return POOL_TILE + 6 * g + (6 if second else 2)
    if n < FIN_CHUNK:
        return PP_TILE + 2 * (n - PP_CHUNK + 1)
    return FIN_TILE + 4 * (n - FIN_CHUNK + 1)


def ge(eng, sem, value):
    if not isinstance(value, int) or value > 0:
        eng.wait_ge(sem, value)


class Steps:

    def __init__(self, eng, sem):
        self.eng, self.sem, self.n = eng, sem, 0

    def did(self, ins):
        ins.then_inc(self.sem, 1)
        self.n = self.n + 1

    def settle(self):
        ge(self.eng, self.sem, self.n)

    def loop(self, i, first, per):
        self.base = self.n
        self.n = (i - first) * per + self.base

    def leave(self, count, per):
        self.n = self.base + count * per


def att_round(kind, u):
    if kind == "S":
        return 0 if isinstance(u, int) and u == 0 else u * 5 - 3
    if kind == "T":
        last = isinstance(u, int) and u == PBLK * NKV - 1
        return u * 5 + (2 if last else 4)
    return u * 5 + (4 if isinstance(u, int) and u == PBLK * NKV - 1 else 6)


ATT_ROUNDS = 5 * PBLK * NKV


def att_bank(kind, m, first=False):
    if first:
        return 6
    return 6 + {"S": m + 1, "T": m, "V": m}[kind] % 2


def consts():
    j = np.arange(P)
    cur = np.where(j[None, :] <= j[:, None], 0.0, NEG)
    prev = np.where(j[None, :] >= j[:, None], 0.0, NEG)
    none = np.full((P, P), NEG)
    masks = np.stack([np.concatenate(x, 1) for x in ((cur, none), (prev, cur), (cur, prev))], 1)
    row = np.arange(P)
    b, t = (row % NS) // NT, row % NT
    smask = np.full((P, NB + 1, P), NEG)
    for at, seq in enumerate(SEQ_ORDER):
        smask[:, at] = np.where((b[:, None] == seq) & (j[None, :] >= t[:, None]), 0.0, NEG)
    n = np.arange(NS)
    smask[:, NB, :NS] = np.where((b[:, None] == n[None, :] // NT) & (n[None, :] % NT <= t[:, None]), 0.0, NEG)
    smask = smask.reshape(P, -1)[:, :T]
    inv = (np.float32(500000.0) ** (-np.arange(0, 16, 2, dtype=np.float32) / np.float32(16))).astype(np.float32)
    pos = (np.arange(PBLK + 1)[None, :] * P + j[:, None]).astype(np.float32)
    pos[:, PBLK] = 2048 + j % NT
    ang = (pos[:, :, None] * inv).astype(np.float32).astype(np.float64)
    ang = np.repeat(ang, 2, axis=1)
    rc = np.broadcast_to(1.0 / (np.arange(HIST) + 1.0), (P, HIST))
    parts = (np.eye(P), np.cos(ang).reshape(P, -1), np.sin(ang).reshape(P, -1), rc)
    small = np.concatenate(parts, 1)
    return (np.ascontiguousarray(small, np.float32), np.ascontiguousarray(masks.reshape(P, -1), np.float32),
            np.ascontiguousarray(smask, np.float32))


CONST_W = P + 2 * 18 * 8 + HIST
PARAM_W = 8 + 8 + 64 + 64 + 16 + 4


def build(nc, xp, xs, cache_k, cache_v, state, pp, ps_, params, w_in, pool_map, w_pp, w_pa, w_out, w_ple,
          w_gate, const, masks, smask, y_p, y_s, nk_p, nv_p, npool_p, nk_s, nv_s, npool_s):
    with ExitStack() as ctx:
        def sb(name, shape, dt=F32, scope=ctx):
            return scope.enter_context(nc.sbuf_tensor(name, shape, dt))

        def sem(name):
            return ctx.enter_context(nc.semaphore(name))

        def dram(name, shape, dt=F32):
            return nc.dram_tensor(name, shape, dt, kind="Internal").ap()

        xT_d = dram("xT_d", (KT, P, T))
        gate_d = dram("gate_d", (2 * KT, P, T))
        yb_d = dram("yb_d", (KT, P, T))
        qT_d = dram("qT_d", (NH, P, T))
        kT_d = dram("kT_d", (NKV, 2, P, T))
        v_d = dram("v_d", (PBLK + 1, P, NKV, 2 * P))

        m_hi, m_lo = sb("m_hi", [P, KT, T], F32R), sb("m_lo", [P, KT, T], F32R)
        sa = sb("sa", [P, KT, T])
        saf = sa[:].rearrange("p k n -> p (k n)")
        w_hi = sb("w_hi", [P, 2, KT + XKT, WC], F32R)
        w_lo = sb("w_lo", [P, 2, KT + XKT, WC], F32R)
        raw = [sb("raw_a", [P, 4, WC]), sb("raw_b", [P, 4, WC]), sb("raw_c", [P, XKT, WC])]
        par_s = sb("par_s", [P, PARAM_W])
        con_s = sb("con_s", [P, CONST_W])
        hist = sb("hist", [P, KT, NB * HIST])
        w_one = sb("w_one", [P, 1])
        kv_out = sb("kv_out", [P, 2, 2 * NKV * HD])
        g8, ps8, qg, kg, sinks, sinks_s = (par_s[:, a:b] for a, b in
                                          ((0, 8), (8, 16), (16, 80), (80, 144), (144, 160), (160, 164)))
        ident = con_s[:, 0:P]
        cosv = con_s[:, P:P + 144].rearrange("p (a c) -> p a c", c=8)
        sinv = con_s[:, P + 144:P + 288].rearrange("p (a c) -> p a c", c=8)
        rcv = con_s[:, P + 288:P + 288 + HIST]

        with ExitStack() as s0:
            xr = sb("xr", [P, PBLK + 1, D], scope=s0)
            rbc = sb("rbc", [P, T], scope=s0)
            xst = sb("xst", [P, 2, T], scope=s0)
            rs = sb("rs", [P, 4, PBLK + 1], scope=s0)
        with ExitStack() as s1:
            qkst = sb("qkst", [P, 4, T], F32R, scope=s1)
            stack = sb("stack", [P, (PBLK + 1) * 512], F32R, scope=s1)
            hs = sb("hs", [P, 4, 18], scope=s1)
        with ExitStack() as s4:
            kc = sb("kc", [P, 2, NB, HD], scope=s4)
            kts = sb("kts", [P, NB // 2 * P], scope=s4)
            q_even, q_odd = sb("q_even", [P, NH * NS], scope=s4), sb("q_odd", [P, NH * NS], scope=s4)
            k_new, k_low = sb("k_new", [P, NKV * NS], scope=s4), sb("k_low", [P, NKV * NS], scope=s4)
            smsk = sb("smsk", [P, T], scope=s4)
            spt = sb("spt", [P, NB + 1, P], scope=s4)
            vc = sb("vc", [P, 2, NB, 2, HD], scope=s4)
            v_new = sb("v_new", [P, NKV, 2 * P], scope=s4)
            s_out = sb("s_out", [P, KT, NS], scope=s4)
            q_group, v_group = sb("q_group", [P, 2, P], scope=s4), sb("v_group", [P, 2 * P], scope=s4)
            s_gap = sb("s_gap", [P, 160], scope=s4)
            sst = sb("sst", [P, 8], scope=s4)
            sprob = sb("sprob", [P, T], scope=s4)
        with ExitStack() as s3:
            qt = sb("qt", [P, 2, G, P], F32R, scope=s3)
            kt = sb("kt", [P, NKV, 2, 2, P], F32R, scope=s3)
            msk = sb("msk", [P, 3, 2 * P], scope=s3)
            vt = sb("vt", [P, 2, NKV, 2 * P], F32R, scope=s3)
            prob = sb("prob", [P, 2, G, 2 * P], scope=s3)
            pt_hi = sb("pt_hi", [P, 2, G * P], F32R, scope=s3)
            pt_lo = sb("pt_lo", [P, 2, G * P], F32R, scope=s3)
            st = sb("st", [P, 2, 6, G], scope=s3)
            gst = sb("gst", [P, 2, T], scope=s3)
        with ExitStack() as s5:
            ub = sb("ub", [P, 2, UL], scope=s5)
            wa, wb = sb("wa", [P, UL], scope=s5), sb("wb", [P, UL], scope=s5)
            r_hi, r_lo = sb("r_hi", [P, 2, T], F32R, scope=s5), sb("r_lo", [P, 2, T], F32R, scope=s5)
            zs = sb("zs", [P, 2, T], scope=s5)
            keep = sb("keep", [P, 2, NB * HIST], scope=s5)
            pst = sb("pst", [P, 2, P], scope=s5)
        gin = sb("gin", [P, 2, T])
        with ExitStack() as s6:
            mix = sb("mix", [P, KT, T], scope=s6)
            gtmp = sb("gtmp", [P, T], scope=s6)
        with ExitStack() as s7:
            p_hi, p_lo = sb("p_hi", [P, 2, T], F32R, scope=s7), sb("p_lo", [P, 2, T], F32R, scope=s7)
            yrow = sb("yrow", [P, PBLK + 1, WC], scope=s7)
            sg = sb("sg", [P, T], scope=s7)
            yt = sb("yt", [P, 2, T], scope=s7)

        ps = ctx.enter_context(nc.psum_tensor("ps", [P, 8, 512], F32))
        psf = ps[:].rearrange("p b n -> p (b n)")

        def pset(n):
            return ps[:, 3 * (n % 2):3 * (n % 2) + 3, 0:CH]

        def flat(n, w=T):
            return psf[:, 1536 * (n % 2):1536 * (n % 2) + w]

        def thirds(ap):
            return ap.rearrange("p (c n) -> p c n", c=NCH)

        par_loaded, con_loaded, hist_loaded = sem("par_loaded"), sem("con_loaded"), sem("hist_loaded")
        x_loaded = [sem(f"x_loaded{t}") for t in range(PBLK + 1)]
        raw_loaded = [sem(f"raw_loaded{i}") for i in range(3)]
        raw_hi = sem("raw_hi")
        piece_split = [sem(f"piece_split{i}") for i in range(3)]
        tile_done = sem("tile_done")
        set_free = [sem("set_free0"), sem("set_free1")]
        m_used = sem("m_used")
        m_hi_done, m_ready = sem("m_hi_done"), sem("m_ready")
        ssq_done, ms_done, std_done, diag_done = (
            sem("ssq_done"), sem("ms_done"), sem("std_done"), sem("diag_done"))
        xt_copied = sem("xt_copied")
        xt_stored = [sem("xt_stored0"), sem("xt_stored1")]
        dve_step = sem("dve_step")
        round_done, round_free = sem("round_done"), sem("round_free")
        hms_done, hstd_done, stack_done = sem("hms_done"), sem("hstd_done"), sem("stack_done")
        qk_stored, v_stored, kv_kept = sem("qk_stored"), sem("v_stored"), sem("kv_kept")
        gate_stored = [sem("gate_stored0"), sem("gate_stored1")]
        samp_done, samp_out = sem("samp_done"), sem("samp_out")
        q_loaded, smask_loaded, v_new_loaded = sem("q_loaded"), sem("smask_loaded"), sem("v_new_loaded")
        kc_loaded = [sem("kc_loaded0"), sem("kc_loaded1")]
        vc_loaded = [sem("vc_loaded0"), sem("vc_loaded1")]
        key_copied, s_read, s_shift, s_exp, s_prob, spt_copied = (
            sem("key_copied"), sem("s_read"), sem("s_shift"), sem("s_exp"), sem("s_prob"), sem("spt_copied"))
        att_done, att_read = sem("att_done"), sem("att_read")
        masks_loaded, zero_done = sem("masks_loaded"), sem("zero_done")
        unit_loaded = [sem(f"unit_loaded{i}") for i in range(NKV)]
        v_loaded = [sem(f"v_loaded{i}") for i in range(NKV)]
        shift_done, exp_done, prob_done, pt_hi_done = (
            sem("shift_done"), sem("exp_done"), sem("prob_done"), sem("pt_hi_done"))
        yb_stored, yb_loaded = sem("yb_stored"), sem("yb_loaded")
        r_ready, keep_ready, pool_t, pool_copied, pool_stored = (
            sem("r_ready"), sem("keep_ready"), sem("pool_t"), sem("pool_copied"), sem("pool_stored"))
        gin_loaded = [sem("gin_loaded0"), sem("gin_loaded1")]
        p_loaded, p_round, p_round_free = sem("p_loaded"), sem("p_round"), sem("p_round_free")
        yt_done, y_round, y_round_free, y_stored = (
            sem("yt_done"), sem("y_round"), sem("y_round_free"), sem("y_stored"))
        out_stored = sem("out_stored")
        ssq_init, rows_init, mix_ready, p_half = (
            sem("ssq_init"), sem("rows_init"), sem("mix_ready"), sem("p_half"))

        nh = NB * HIST
        ones = saf[:, 1280:1280 + P]
        rows = saf[:, 2880:2880 + 2 * (PBLK + 1) * P].rearrange("p (s n) -> p s n", s=2)
        m_hi32, m_lo32 = m_hi[:].bitcast(F32), m_lo[:].bitcast(F32)
        st32 = stack[:].bitcast(F32)
        q_stack = st32[:, 0:2304].rearrange("p (b h e) -> p b h e", h=2, e=P)
        k_stack = st32.rearrange("p (b s e) -> p b s e", s=4, e=P)
        pt_hi32, r_hi32, p_hi32 = (x[:].bitcast(F32) for x in (pt_hi, r_hi, p_hi))

        def tile_free(eng, n):
            ge(eng, set_free[n % 2], n // 2 + 1)

        block = ctx.enter_context(nc.Block())

        @block.sync
        def _(sp):
            def load_chunk(n, w, col, extra=None, extra_n=None):
                for h in range(2):
                    ge(sp, piece_split[h], n)
                    src = w[512 * h:512 * h + 512, bass.ds(col, WC)].rearrange("(k p) n -> p k n", p=P)
                    sp.dma_start(raw[h][:], src).then_inc(raw_loaded[h], 16)
                if extra is not None:
                    ge(sp, piece_split[2], extra_n)
                    sp.dma_start(raw[2][:], extra.rearrange("(k p) n -> p k n", p=P)).then_inc(raw_loaded[2], 16)

            sp.dma_start(con_s[:], const).then_inc(con_loaded, 16)
            sp.dma_start(par_s[:], params).then_inc(par_loaded, 16)
            for t in range(PBLK):
                sp.dma_start(xr[:, t, :], xp[P * t:P * t + P, :]).then_inc(x_loaded[t], 16)
            sp.dma_start(xr[0:NS, PBLK, :], xs).then_inc(x_loaded[PBLK], 16)
            sp.dma_start(saf[0:NB * HIST, 4096:4096 + D], state).then_inc(hist_loaded, 16)

            load_chunk(0, w_in, COL["q"])
            with sp.Fori(1, 6) as c:
                load_chunk(c, w_in, c * WC + COL["q"])
            for b in range(NB):
                for new, old in ((nk_s, cache_k), (nv_s, cache_v)):
                    sp.dma_start(new[b, 0:P - NT, :], old[b, NT:P, :]).then_inc(out_stored, 16)
            for n in range(GATE_CHUNK, GATE_CHUNK + 2):
                load_chunk(n, w_in, (n - GATE_CHUNK) * WC + COL["za"])

            ck = cache_k.rearrange("b j (v d) -> v j b d", v=NKV)
            cv = cache_v.rearrange("b j (v d) -> v j b d", v=NKV)
            sp.wait_ge(qk_stored, 16 * 10)
            sp.dma_start(kc[:, 0], ck[0]).then_inc(kc_loaded[0], 16)
            for half in range(2):
                for part, dst in ((0, q_even), (1, q_odd)):
                    src = qT_d[:, HD * part:HD * part + HD, SEQ:T].rearrange("h p n -> p h n")
                    sp.dma_start(dst[HD * half:HD * half + HD, :].rearrange("p (h n) -> p h n", n=NS), src)\
                        .then_inc(q_loaded, 16)
            for part, dst in ((0, k_new), (1, k_low)):
                sp.dma_start(dst[:].rearrange("p (v n) -> p v n", n=NS),
                             kT_d[:, part, :, SEQ:T].rearrange("v p n -> p v n")).then_inc(q_loaded, 16)
            sp.dma_start(smsk[:], smask).then_inc(smask_loaded, 16)
            sp.dma_start(kc[:, 1], ck[1]).then_inc(kc_loaded[1], 16)
            sp.wait_ge(v_stored, 16 * 2)
            sp.dma_start(v_new[0:NS], v_d[PBLK, 0:NS]).then_inc(v_new_loaded, 16)
            for g in range(2):
                for c in range(2):
                    sp.dma_start(vc[:, g, :, c, :], cv[g]).then_inc(vc_loaded[g], 16)
            sp.wait_ge(kv_kept, 4)
            sp.dma_start(nk_p, kv_out[:, 0, 0:256]).then_inc(out_stored, 16)
            sp.dma_start(nv_p, kv_out[:, 0, 256:512]).then_inc(out_stored, 16)
            for b in range(NB):
                sp.dma_start(nk_s[b, P - NT:P, :], kv_out[NT * b:NT * b + NT, 1, 0:256]).then_inc(out_stored, 16)
                sp.dma_start(nv_s[b, P - NT:P, :], kv_out[NT * b:NT * b + NT, 1, 256:512]).then_inc(out_stored, 16)
            for g in range(2, NKV):
                load_chunk(GATE_CHUNK + g, w_in, g * WC + COL["za"])
                sp.wait_ge(key_copied, g - 1)
                sp.dma_start(kc[:, g % 2], ck[g]).then_inc(kc_loaded[g % 2], 16)
                sp.wait_ge(samp_out, g)
                for c in range(2):
                    sp.dma_start(vc[:, g % 2, :, c, :], cv[g]).then_inc(vc_loaded[g % 2], 16)
            for n in range(GATE_CHUNK + 4, GATE_CHUNK + 6):
                load_chunk(n, w_in, (n - GATE_CHUNK) * WC + COL["za"])

            def load_q_k(u, t, m):
                tok, kv = bass.ds(t * P, P), m % 4
                sp.dma_start(qt[:, m % 2, :, :].bitcast(F32),
                             qT_d[G * kv:G * kv + G, :, tok].rearrange("g p n -> p g n")).then_inc(unit_loaded[kv], 16)
                sp.dma_start(kt[:, kv, :, m // 4, :].bitcast(F32),
                             kT_d[kv, :, :, tok].rearrange("h p n -> p h n")).then_inc(unit_loaded[kv], 16)

            def load_v(t, m):
                sp.dma_start(vt[:, m // 4, m % 4, :].bitcast(F32), v_d[t, :, m % 4, :]).then_inc(v_loaded[m % 4], 16)

            def load_unit(i, m):
                u, t = 8 * i + m, 2 * i + m // 4
                sp.wait_ge(att_done, att_round("S", u - 2) + 2)
                load_q_k(u, t, m)
                load_v(t, m)

            sp.wait_ge(s_read, 3 * NKV)
            sp.dma_start(msk[:].rearrange("p a n -> p (a n)"), masks).then_inc(masks_loaded, 16)
            for m in range(2):
                load_q_k(m, 0, m)
            sp.wait_ge(zero_done, 2)
            for m in range(2):
                load_v(0, m)

            def load_units(i, chunk_a, chunk_b):
                for m in range(2, 8):
                    load_unit(i, m)
                    if m == 2:
                        load_chunk(*chunk_a)
                    if m == 6:
                        load_chunk(*chunk_b)

            def gate_chunk(n):
                return n, w_in, (n - GATE_CHUNK) * WC + COL["za"]

            load_units(0, gate_chunk(GATE_CHUNK + 6), gate_chunk(GATE_CHUNK + 7))
            with sp.Fori(1, 3) as i:
                for m in range(2):
                    load_unit(i, m)
                load_units(i, gate_chunk(i * 2 + (GATE_CHUNK + 6)), gate_chunk(i * 2 + (GATE_CHUNK + 7)))
            for m in range(2):
                load_unit(3, m)
            load_units(3, (POOL_CHUNK, w_in, 0), (POOL_CHUNK + 1, w_in, COL["zp"], pool_map[0], 0))
            sp.wait_ge(att_read, ATT_ROUNDS)
            sp.dma_start(yb_d.rearrange("k p n -> p k n"), sa[:]).then_inc(yb_stored, 16)

            with sp.Fori(1, 4) as g:
                load_chunk(g * 2 + POOL_CHUNK, w_in, g * WC)
                load_chunk(g * 2 + POOL_CHUNK + 1, w_in, g * WC + COL["zp"], pool_map[g], g)

            def stage(base, chunk, w, src):
                with sp.Fori(0, 4) as c:
                    load_chunk(c + chunk, w, c * WC)
                    for h in range(2):
                        sp.wait_ge(set_free[h], c + base // 2)
                        sp.dma_start(gin[:, h, :], src[c * 2 + h]).then_inc(gin_loaded[h], 16)

            stage(PP_TILE, PP_CHUNK, w_pp, gate_d)
            sp.wait_ge(m_ready, 2 * KT)
            sp.wait_ge(yb_stored, 16)
            sp.dma_start(sa[:], yb_d.rearrange("k p n -> p k n")).then_inc(yb_loaded, 16)
            stage(PA_TILE, PA_CHUNK, w_pa, gate_d[KT:2 * KT])
            for h in range(2):
                sp.wait_ge(xt_stored[h], 16 * (KT // 2))
            stage(WO_TILE, WO_CHUNK, w_out, xT_d)
            sp.wait_ge(m_ready, 4 * KT)
            for t in range(PBLK):
                sp.dma_start(yrow[:, t, :], pp[P * t:P * t + P, :]).then_inc(p_loaded, 16)
            sp.dma_start(yrow[0:NS, PBLK, :], ps_).then_inc(p_loaded, 16)
            load_chunk(FIN_CHUNK, w_gate, 0, w_ple[:, 0:WC], 4)
            with sp.Fori(1, 4) as c:
                load_chunk(c + FIN_CHUNK, w_gate, c * WC, w_ple[:, bass.ds(c * WC, WC)], c + 4)
            sp.wait_ge(out_stored, 16 * (2 * NB + 2 + 2 * NB))

        @block.gpsimd
        def _(pool):
            hi_count = Steps(pool, raw_hi)
            hi_count.did(nc.gpsimd.memset(w_one[:], 1.0))
            hi_count.settle()

            def split(n, slot, end, piece, k0, kn, m):
                pool.wait_ge(raw_loaded[piece], (m + 1) * 16)
                ge(pool, tile_done, end)
                hi, lo = w_hi[:, slot, k0:k0 + kn, :], w_lo[:, slot, k0:k0 + kn, :]
                one = w_one[:, 0:1].unsqueeze(2).to_broadcast([P, kn, WC])
                hi_count.did(nc.gpsimd.tensor_tensor(hi, raw[piece][:], one, ALU.mult))
                hi_count.settle()
                nc.gpsimd.tensor_tensor(lo, raw[piece][:], hi.bitcast(F32), ALU.subtract)\
                    .then_inc(piece_split[piece], 1)

            def chunk(n, slot, end, m=None):
                split(n, slot, end, 0, 0, 4, n)
                split(n, slot, end, 1, 4, 4, n)
                if m is not None:
                    split(n, slot, end, 2, KT, XKT, m)

            def chunks(first, count, per_pair, steps, extra=None):
                for h in range(2):
                    n = first + h
                    chunk(n, h, chunk_end(n - 2) if n >= 2 else 0, extra(0, h) if extra else None)
                with pool.Fori(1, count // 2) as i:
                    hi_count.loop(i, 1, steps)
                    for h in range(2):
                        done = i * per_pair + (chunk_end(first + h) - per_pair)
                        chunk(i * 2 + (first + h), h, done, extra(i, h) if extra else None)
                hi_count.leave(count // 2 - 1, steps)

            chunks(QKV_CHUNK, 6, 4, 4)
            chunks(GATE_CHUNK, 12, 4, 4)
            chunks(POOL_CHUNK, 8, 6, 5, lambda i, h: i if h else None)
            chunks(PP_CHUNK, 4, 4, 4)
            chunks(PA_CHUNK, 4, 4, 4)
            chunks(WO_CHUNK, 4, 4, 4)
            chunks(FIN_CHUNK, 4, 8, 6, lambda i, h: i * 2 + (4 + h))

        @block.tensor
        def _(pe):
            def project(parity, free, slot, f, src_hi, src_lo, wait_m=None, used=False, k0=0, kn=KT,
                        pieces=None, after=None, done=False):
                ge(pe, set_free[parity], free)
                for k in range(kn):
                    for at, sem_, value in pieces or ():
                        if at == k:
                            pe.wait_ge(sem_, value)
                    if wait_m is not None:
                        pe.wait_ge(m_ready, wait_m + (k + 1))
                    wh = w_hi[:, slot, k0 + k, P * f:P * f + P]
                    wl = w_lo[:, slot, k0 + k, P * f:P * f + P]
                    for w, parts in ((wh, (src_hi, src_lo)), (wl, (src_hi,))):
                        for c in range(NCH):
                            for x in parts:
                                last = nc.tensor.matmul(
                                    ps[:, 3 * parity + c, 0:CH], w, x[:, k, CH * c:CH * c + CH],
                                    start=(k == 0 and w is wh and x is src_hi),
                                    stop=(k == kn - 1 and w is wl))
                    if used and k < kn - 1:
                        last.then_inc(m_used, 1)
                    if done and k == kn - 1:
                        last.then_inc(tile_done, 1)
                    for call in (after or {}).get(k, ()):
                        call()
                return last

            def ab(n):
                return ((0, piece_split[0], n + 1), (4, piece_split[1], n + 1))

            pe.wait_ge(con_loaded, 16)
            pe.wait_ge(diag_done, 1)
            for t in range(PBLK + 1):
                w = P if t < PBLK else NS
                last = nc.tensor.matmul(flat(0)[:, P * t:P * t + w], ones[0:w, :], saf[0:w, P * t:P * t + w],
                                        start=True, stop=True)
            last.then_inc(tile_done, 1)
            pe.wait_ge(hist_loaded, 16)
            nh = NB * HIST
            for k in range(KT):
                last = nc.tensor.transpose(ps[:, 3 + k // 4, nh * (k % 4):nh * (k % 4) + nh],
                                           saf[0:nh, 4096 + P * k:4096 + P * k + P], ident[0:nh, 0:nh])
            last.then_inc(tile_done, 1)
            for k in range(KT):
                n = X_TILE + k
                ge(pe, set_free[n % 2], n // 2)
                for t in range(PBLK + 1):
                    w = P if t < PBLK else NS
                    last = nc.tensor.transpose(flat(n)[:, P * t:P * t + w], xr[0:w, t, P * k:P * k + P],
                                               ident[0:w, 0:w])
                last.then_inc(tile_done, 1)

            def turn(kind, j, i, r):
                ge(pe, round_free, r - 1)
                bank = 6 + r % 2
                if kind == "rows":
                    if i == 0:
                        ge(pe, set_free[j % 2], (QKV_TILE + j) // 2 + 1)
                    for b in range(4 if i < 2 else 0):
                        last = nc.tensor.transpose(ps[:, bank, P * b:P * b + P],
                                                   saf[:, P * (4 * i + b):P * (4 * i + b) + P], ident)
                    if i == 2:
                        last = nc.tensor.transpose(ps[0:NS, bank, 0:P], saf[:, SEQ:T], ident)
                else:
                    if i == 0:
                        ge(pe, stack_done, j + 1)
                    src = q_stack if kind == "q" else k_stack
                    s = 2 if kind == "q" else 4
                    for b in range(4 if i < 2 * s else 0):
                        last = nc.tensor.transpose(ps[:, bank, P * b:P * b + P],
                                                   src[:, 4 * (i % 2) + b, i // 2, :], ident)
                    for b in range(s if i == 2 * s else 0):
                        last = nc.tensor.transpose(ps[:, bank, NS * b:NS * b + NS], src[0:NS, PBLK, b, :],
                                                   ident[0:NS, 0:NS])
                last.then_inc(round_done, 1)

            for j in range(12):
                after = {}
                for step, kind, jj, i, r in PLAN[j]:
                    after.setdefault(step, []).append(lambda a=(kind, jj, i, r): turn(*a))
                project(j % 2, (QKV_TILE + j) // 2, (j // 2) % 2, j % 2, m_hi, m_lo, wait_m=0 if j == 0 else None,
                        pieces=ab(j // 2), after=after).then_inc(tile_done, 1)
            for _, kind, jj, i, r in PLAN[12]:
                turn(kind, jj, i, r)

            ge(pe, round_free, ROUNDS)

            def turn_keys(i, g):
                pe.wait_ge(kc_loaded[g], i * 16 + 16)
                for p in range(NB // 2):
                    last = nc.tensor.transpose(ps[:, 6, P * p:P * p + P],
                                               kc[:, g, 2 * p:2 * p + 2, :].rearrange("p b e -> p (b e)"), ident)
                last.then_inc(samp_done, 1)

            def sample_scores(v, r):
                if r == 0:
                    pe.wait_ge(samp_out, v + 1)
                    pe.wait_ge(key_copied, v + 1)
                if r == 2:
                    pe.wait_ge(s_read, v * 3 + 1)
                q = q_group[:, r % 2, :]
                keys = kts[:] if r < 2 else k_new[:, bass.ds(v * NS, NS)]
                nc.tensor.matmul(ps[:, (7, 6, 7)[r], 0:(512, 512, NS)[r]], q, keys, start=True, stop=True)\
                    .then_inc(samp_done, 1)

            def turn_sample_probs(v, r):
                if r == 0:
                    pe.wait_ge(s_prob, v + 1)
                if r == 2:
                    pe.wait_ge(spt_copied, v * 3 + 1)
                for b in range(4 * r, min(4 * r + 4, NB + 1)):
                    w = P if b < NB else NS
                    last = nc.tensor.transpose(ps[0:w, (6, 7, 6)[r], P * (b % 4):P * (b % 4) + P],
                                               sprob[:, P * b:P * b + w], ident)
                last.then_inc(samp_done, 1)

            def sample_values(v, i, g):
                pe.wait_ge(spt_copied, v * 3 + 3)
                pe.wait_ge(vc_loaded[g], i * 32 + 32)
                for b, seq in enumerate(SEQ_ORDER):
                    nc.tensor.matmul(ps[:, 7, 0:P], vc[:, g, seq].rearrange("p c e -> p (c e)"), spt[:, b, :],
                                     start=(b == 0), stop=False)
                for part in range(2):
                    last = nc.tensor.matmul(ps[:, 7, 0:P], v_group[0:NS, P * part:P * part + P], spt[0:NS, NB, :], start=False, stop=(part == 1))
                last.then_inc(samp_done, 1)

            with pe.Fori(0, 2) as i:
                for h in range(4):
                    g = h // 2
                    v = i * 2 + g
                    if h % 2 == 0:
                        after = {2: [lambda i=i, g=g: turn_keys(i, g)],
                                 5: [lambda v=v: sample_scores(v, 0), lambda v=v: sample_scores(v, 1)],
                                 6: [lambda v=v: sample_scores(v, 2)]}
                    else:
                        after = {3: [lambda v=v: turn_sample_probs(v, 0), lambda v=v: turn_sample_probs(v, 1)],
                                 4: [lambda v=v: turn_sample_probs(v, 2)],
                                 7: [lambda v=v, i=i, g=g: sample_values(v, i, g)]}
                    project(h % 2, i * 2 + (GATE_TILE // 2 + h // 2), h // 2, h % 2, m_hi, m_lo,
                            pieces=ab(i * 2 + (GATE_CHUNK + h // 2)), after=after, done=True)

            def round_of(kind, u, s, m, first=False):
                r = att_round(kind, u) + s
                if not isinstance(r, int) or r >= 2:
                    pe.wait_ge(att_read, r if kind == "V" else r - 1)
                return 6 + (att_bank(kind, m, first) + s) % 2

            def scores(u, m, t, s, first=False):
                slot, kv = m % 2, m % 4
                if s == 0:
                    pe.wait_ge(unit_loaded[kv], t * 32 + 32)
                bank = round_of("S", u, s, m, first)
                for g in (2 * s, 2 * s + 1):
                    for part in range(2):
                        last = nc.tensor.matmul(ps[:, bank, 256 * (g % 2):256 * (g % 2) + 256], qt[:, slot, g, :],
                                                kt[:, kv, part, :, :].rearrange("p s n -> p (s n)"),
                                                start=(part == 0), stop=(part == 1))
                last.then_inc(att_done, 1)

            def turn_probs(u, m, s):
                if s == 0:
                    pe.wait_ge(prob_done, u + 1)
                bank = round_of("T", u, s, m)
                for g in range(G):
                    last = nc.tensor.transpose(ps[:, bank, P * g:P * g + P], prob[:, m % 2, g, P * s:P * s + P], ident)
                last.then_inc(att_done, 1)

            def values(u, m, t):
                kv = m % 4
                bank = round_of("V", u, 0, m)
                pe.wait_ge(v_loaded[kv], t * 16 + 16)
                for s in range(2):
                    for a, b in ((0, pt_hi), (0, pt_lo), (1, pt_hi)):
                        last = nc.tensor.matmul(ps[:, bank, :], vt[:, s, kv, P * a:P * a + P], b[:, s, :],
                                                start=(s == 0 and a == 0 and b is pt_hi),
                                                stop=(s == 1 and a == 1))
                last.then_inc(att_done, 1)

            def attention_half(i, m, k0, first):
                u, t = i * 8 + m, i * 2 + m // 4
                after = {k0: [], k0 + 1: [], k0 + 2: []}
                if not first or m >= 2:
                    after[k0].append(lambda: values(u - 2, (m - 2) % 8, t if m % 4 >= 2 else t - 1))
                after[k0].append(lambda: scores(u, m, t, 0, first and m < 2))
                after[k0 + 1].append(lambda: scores(u, m, t, 1, first and m < 2))
                if not first or m >= 1:
                    after[k0 + 2] += [lambda: turn_probs(u - 1, (m - 1) % 8, 0), lambda: turn_probs(u - 1, (m - 1) % 8, 1)]
                return after

            def attention_tiles(i, first=False):
                for h in range(4):
                    after = attention_half(i, 2 * h, 0, first) | attention_half(i, 2 * h + 1, 4, first)
                    project(h % 2, i * 2 + ((GATE_TILE + KT) // 2 + h // 2), h // 2, h % 2, m_hi, m_lo,
                            pieces=ab(i * 2 + (GATE_CHUNK + 4 + h // 2)), after=after, done=True)

            pe.wait_ge(spt_copied, 3 * NKV)
            pe.wait_ge(samp_out, NKV + 1)
            pe.wait_ge(zero_done, 2)
            attention_tiles(0, first=True)
            with pe.Fori(1, PBLK // 2) as i:
                attention_tiles(i)

            def turn_history(h, value):
                ge(pe, keep_ready, value)
                pe.wait_ge(pool_copied, value)
                nc.tensor.transpose(ps[0:nh, 6, 0:P], keep[:, h, :], ident)
                nc.tensor.transpose(ps[0:HIST, 6, P:2 * P], ub[:, h, SEQ:SEQ + HIST], ident).then_inc(pool_t, 1)

            def pool_group(g, tail=None):
                half = g * 3 + POOL_TILE // 2
                for h in range(2):
                    project(h, half, 0, h, m_hi, m_lo, pieces=ab(g * 2 + POOL_CHUNK), after=tail if h == 0 else None,
                            done=True)
                for h in range(2):
                    project(h, half + 1, 1, h, m_hi, m_lo, pieces=ab(g * 2 + (POOL_CHUNK + 1)), used=(h == 1),
                            after={3: [lambda h=h: turn_history(h, g * 2 + (h + 1))]}, done=True)
                for h in range(2):
                    pe.wait_ge(r_ready, g * 2 + 2)
                    project(h, half + 2, 1, h, r_hi, r_lo, k0=KT, kn=XKT,
                            pieces=((0, piece_split[2], g + 1),), done=True)

            end = PBLK * NKV
            pool_group(0, {0: [lambda: values(end - 2, 6, PBLK - 1)],
                           2: [lambda: turn_probs(end - 1, 7, 0), lambda: turn_probs(end - 1, 7, 1)],
                           5: [lambda: values(end - 1, 7, PBLK - 1)]})
            with pe.Fori(1, 4) as g:
                pool_group(g)

            def stage(base, chunk, fills):
                with pe.Fori(0, 2) as i:
                    for h in range(4):
                        project(h % 2, i * 2 + (base // 2 + h // 2), h // 2, h % 2, m_hi, m_lo,
                                wait_m=KT * fills if h == 0 else None, used=(h == 3),
                                pieces=ab(i * 2 + (chunk + h // 2))).then_inc(tile_done, 1)

            stage(PP_TILE, PP_CHUNK, 1)
            stage(PA_TILE, PA_CHUNK, 2)
            stage(WO_TILE, WO_CHUNK, 3)

            pe.wait_ge(p_loaded, 16 * (PBLK + 1))
            for r in range(6):
                k, i = divmod(r, 3)
                ge(pe, p_round_free, r - 1)
                for b in range(4 if i < 2 else 0):
                    last = nc.tensor.transpose(ps[:, 6 + r % 2, P * b:P * b + P],
                                               yrow[:, 4 * i + b, P * k:P * k + P], ident)
                if i == 2:
                    last = nc.tensor.transpose(ps[:, 6 + r % 2, 0:NS], yrow[0:NS, PBLK, P * k:P * k + P],
                                               ident[0:NS, 0:NS])
                last.then_inc(p_round, 1)

            def turn_y(h, r, need, i):
                if i == 0:
                    ge(pe, yt_done, need)
                ge(pe, y_round_free, r - 1)
                bank = 6 + (3 * h + i) % 2
                for b in range(4 if i < 2 else 0):
                    t = 4 * i + b
                    last = nc.tensor.transpose(ps[:, bank, P * b:P * b + P], yt[:, h, P * t:P * t + P], ident)
                if i == 2:
                    last = nc.tensor.transpose(ps[0:NS, bank, 0:P], yt[:, h, SEQ:T], ident)
                last.then_inc(y_round, 1)

            def final_chunk(c, slot, first=False):
                for h in range(2):
                    j = c * 2 + h
                    after = {}
                    if not first or h:
                        hh = 1 - h
                        after = {4 + i: [lambda i=i, j=j, hh=hh: turn_y(hh, (j - 1) * 3 + i, j, i)] for i in range(3)}
                    half = c * 2 + (FIN_TILE // 2 + h)
                    project(0, half, slot, h, m_hi, m_lo, wait_m=4 * KT if h == 0 else None,
                            pieces=ab(c + FIN_CHUNK), after=after).then_inc(tile_done, 1)
                    pe.wait_ge(p_round_free, 6)
                    project(1, half, slot, h, p_hi, p_lo, k0=KT, kn=XKT,
                            pieces=((0, piece_split[2], c + 5),)).then_inc(tile_done, 1)

            final_chunk(0, 0, first=True)
            final_chunk(1, 1)
            with pe.Fori(1, 2) as i:
                for h in range(2):
                    final_chunk(i * 2 + h, h)
            for i in range(3):
                turn_y(1, 21 + i, 8, i)

        @block.vector
        def _(dve):
            v = nc.vector
            step = Steps(dve, dve_step)

            def split_lo(k, value):
                dve.wait_ge(m_hi_done, value)
                v.tensor_tensor(m_lo[:, k, :], sa[:, k, :], m_hi32[:, k, :], ALU.subtract).then_inc(m_ready, 1)

            step.did(v.memset(rs[:, 0, :], 1.0))
            step.did(v.memset(ones, 1.0))
            step.settle()
            v.memset(rs[:, 1, :], 1.0).then_inc(ssq_init, 1)
            dve.wait_ge(ssq_done, PBLK + 1)
            v.tensor_scalar(rs[:, 1, :], rs[:, 0, :], 1.0 / D, EPS, ALU.mult, ALU.add).then_inc(ms_done, 1)
            dve.wait_ge(std_done, 1)
            step.did(v.reciprocal(rs[:, 3, :], rs[:, 2, :]))
            step.settle()
            dve.wait_ge(con_loaded, 16)
            for t in range(PBLK + 1):
                last = v.tensor_scalar(saf[:, P * t:P * t + P], ident, rs[:, 3, t:t + 1], None, ALU.mult)
            last.then_inc(diag_done, 1)
            dve.wait_ge(tile_done, 1)
            step.did(v.tensor_copy(rbc[:], flat(0)))
            v.memset(rs[:, 1, 0:1], 0.0).then_inc(set_free[0], 1)
            step.settle()
            dve.wait_ge(par_loaded, 16)
            for k in range(KT):
                dve.wait_ge(xt_copied, k + 1)
                v.scalar_tensor_tensor(sa[:, k, :], flat(k), g8[:, k:k + 1], rbc[:], ALU.mult, ALU.mult)\
                    .then_inc(set_free[k % 2], 1)
                if k:
                    split_lo(k - 1, k)
            split_lo(KT - 1, KT)

            step.did(v.tensor_scalar(qg, qg, HD ** -0.5, None, ALU.mult))
            dve.wait_ge(m_ready, KT)
            for h in range(2):
                dve.wait_ge(xt_stored[h], 16 * (KT // 2))
            v.memset(rows[:, :, PBLK * P:], 1.0).then_inc(rows_init, 1)
            step.settle()
            sq = saf[:, 1056:1056 + 1152].rearrange("p (a e) -> p a e", e=HD)
            tmp = [saf[:, 2304 + 144 * i:2304 + 144 * i + 144].rearrange("p (a e) -> p a e", e=8) for i in range(4)]

            def heads(par):
                return rows[:, par, :].rearrange("p (a e) -> p a e", e=HD)

            def stack_free(j):
                if 1 <= j <= 10:
                    dve.wait_ge(round_done, BACK_END[j - 1])
                elif j == 11:
                    dve.wait_ge(v_stored, 16)

            def keep_kv(j):
                col = P * (j - 8)
                v.tensor_copy(kv_out[:, 0, col:col + P], rows[:, j % 2, 7 * P:8 * P])
                v.tensor_copy(kv_out[0:NS, 1, col:col + P], rows[0:NS, j % 2, 8 * P:9 * P]).then_inc(kv_kept, 1)

            def dup_stack(j):
                x = heads(j % 2).unsqueeze(2).to_broadcast([P, 18, 2, HD])
                out = [stack[:].rearrange("p (a s c e) -> p a s c e", s=2, c=2, e=HD)[:, :, s] for s in range(2)]
                hi32 = st32.rearrange("p (a s c e) -> p a s c e", s=2, c=2, e=HD)[:, :, 0]
                stack_free(j)
                step.did(v.tensor_copy(out[0], x))
                step.settle()
                v.tensor_tensor(out[1], x, hi32, ALU.subtract).then_inc(stack_done, 1)

            for j in range(12):
                x = heads(j % 2)
                dve.wait_ge(round_free, ROWS_END[j])
                if j < 10:
                    step.did(v.tensor_tensor(sq, x, x, ALU.mult))
                    step.settle()
                    step.did(v.tensor_reduce(hs[:, 0, :], sq, AX_X, ALU.add))
                    step.settle()
                    v.tensor_scalar(hs[:, 1, :], hs[:, 0, :], 1.0 / HD, EPS, ALU.mult, ALU.add).then_inc(hms_done, 1)
                    gain = (qg if j < 8 else kg).unsqueeze(1).to_broadcast([P, 18, HD])
                    step.did(v.tensor_tensor(x, x, gain, ALU.mult))
                    dve.wait_ge(hstd_done, j + 1)
                    step.did(v.reciprocal(hs[:, 3, :], hs[:, 2, :]))
                    step.settle()
                    step.did(v.tensor_tensor(x, x, hs[:, 3, :].unsqueeze(2).to_broadcast([P, 18, HD]), ALU.mult))
                    step.settle()
                    x1, x2 = x[:, :, 0:8], x[:, :, 8:16]
                    for o, a, b in zip(tmp, (x1, x2, x2, x1), (cosv, sinv, cosv, sinv)):
                        last = v.tensor_tensor(o, a, b, ALU.mult)
                    step.did(last)
                    step.settle()
                    v.tensor_tensor(x1, tmp[0], tmp[1], ALU.subtract)
                    step.did(v.tensor_tensor(x2, tmp[2], tmp[3], ALU.add))
                    step.settle()
                if j >= 8:
                    keep_kv(j)
                    dup_stack(j)
                else:
                    hi, lo = (stack[:, 0:2304].rearrange("p (a s e) -> p a s e", s=2, e=HD)[:, :, s] for s in (0, 1))
                    hi32 = st32[:, 0:2304].rearrange("p (a s e) -> p a s e", s=2, e=HD)[:, :, 0]
                    stack_free(j)
                    step.did(v.tensor_copy(hi, x))
                    step.settle()
                    v.tensor_tensor(lo, x, hi32, ALU.subtract).then_inc(stack_done, 1)

            dve.wait_ge(q_loaded, 16 * 6)
            step.did(v.tensor_tensor(q_even[:], q_even[:], q_odd[:], ALU.add))
            step.did(v.tensor_tensor(k_new[:], k_new[:], k_low[:], ALU.add))
            step.settle()
            step.did(v.tensor_copy(q_odd[HD:P, :], q_even[HD:P, :]))
            step.settle()
            v.memset(q_odd[0:HD, :], 0.0)
            v.memset(q_even[HD:P, :], 0.0).then_inc(samp_out, 1)
            dve.wait_ge(smask_loaded, 16)
            with dve.Fori(0, NKV) as kv:
                step.loop(kv, 0, 6)
                ge(dve, samp_done, kv * 8 + 2)
                for r, (bank, c0, w) in enumerate(((7, 0, 512), (6, 512, 512), (7, SEQ, NS))):
                    if r:
                        dve.wait_ge(samp_done, kv * 8 + (2 + r))
                    v.tensor_tensor(sprob[:, c0:c0 + w], ps[:, bank, 0:w], smsk[:, c0:c0 + w], ALU.add)\
                        .then_inc(s_read, 1)
                dve.wait_ge(s_read, kv * 3 + 3)
                step.did(v.tensor_reduce(sst[:, 0:1], sprob[:], AX_X, ALU.max))
                step.did(v.tensor_copy(sst[:, 7:8], sinks_s[:, bass.ds(kv, 1)]))
                step.settle()
                step.did(v.tensor_tensor(sst[:, 6:7], sst[:, 0:1], sst[:, 7:8], ALU.max))
                step.settle()
                v.tensor_scalar(sst[:, 1:2], sst[:, 6:7], -1.0, None, ALU.mult)
                v.tensor_tensor(sst[:, 2:3], sst[:, 7:8], sst[:, 6:7], ALU.subtract).then_inc(s_shift, 1)
                dve.wait_ge(s_exp, kv + 1)
                step.did(v.tensor_tensor(sst[:, 5:6], sst[:, 3:4], sst[:, 4:5], ALU.add))
                step.settle()
                step.did(v.reciprocal(sst[:, 6:7], sst[:, 5:6]))
                step.settle()
                v.tensor_scalar(sprob[:], sprob[:], sst[:, 6:7], None, ALU.mult).then_inc(s_prob, 1)
                dve.wait_ge(samp_done, kv * 8 + 8)
                for q in range(2):
                    half = slice(64 * q, 64 * q + 64)
                    o = ps[half, 7, 0:P].rearrange("p (a q n) -> p q a n", q=2, n=NS)[:, q]
                    last = v.tensor_copy(s_out[half, bass.ds(kv * 2, 2), :], o)
                last.then_inc(samp_out, 1)
                step.did(v.memset(sst[:, 0:1], 0.0))
            step.leave(NKV, 6)
            v.memset(kt[:, :, :, 1, :].bitcast(F32), 0.0).then_inc(zero_done, 1)
            tile_free(dve, GATE_TILE + 6)
            tile_free(dve, GATE_TILE + 7)
            dve.wait_ge(samp_out, NKV + 1)
            step.did(v.tensor_tensor(sa[:, :, SEQ:T], sa[:, :, SEQ:T], s_out[:], ALU.mult))
            step.settle()
            v.memset(vt[:, 1, :, :].bitcast(F32), 0.0).then_inc(zero_done, 1)

            dve.wait_ge(masks_loaded, 16)
            dve.wait_ge(zero_done, 2)

            def mask_scores(u, m, mask, first):
                slot, kv = m % 2, m % 4
                for s in range(2):
                    n = att_round("S", u) + s + 1
                    dve.wait_ge(att_done, n)
                    v.tensor_copy(st[:, slot, 5, 2 * s:2 * s + 2], sinks[:, G * kv + 2 * s:G * kv + 2 * s + 2])
                    for g in (2 * s, 2 * s + 1):
                        bank = 6 + (att_bank("S", m, first) + s) % 2
                        last = v.tensor_tensor_reduce(
                            prob[:, slot, g, :], ps[:, bank, 256 * (g % 2):256 * (g % 2) + 256],
                            msk[:, mask, :], 1.0, sinks[:, G * kv + g:G * kv + g + 1], ALU.add, ALU.max,
                            st[:, slot, 0, g:g + 1])
                    last.then_inc(att_read, 1)
                dve.wait_ge(att_read, n)
                v.tensor_scalar(st[:, slot, 1, :], st[:, slot, 0, :], -1.0, None, ALU.mult)
                v.tensor_tensor(st[:, slot, 2, :], sinks[:, G * kv:G * kv + G], st[:, slot, 0, :], ALU.subtract)\
                    .then_inc(shift_done, 1)

            def split_probs(u, m):
                for s in range(2):
                    ge(dve, pt_hi_done, u * 2 + (s + 1))
                    bank = 6 + (att_bank("T", m) + s) % 2
                    v.tensor_tensor(pt_lo[:, s, :], ps[:, bank, :], pt_hi32[:, s, :], ALU.subtract)\
                        .then_inc(att_read, 1)

            def gate_output(u, m, tok):
                kv = m % 4
                dve.wait_ge(att_done, att_round("V", u) + 1)
                for q in range(2):
                    half = slice(64 * q, 64 * q + 64)
                    o = ps[half, att_bank("V", m), :].rearrange("p (a q n) -> p q a n", q=2, n=P)[:, q]
                    dst = sa[half, 2 * kv:2 * kv + 2, tok]
                    last = v.tensor_tensor(dst, o, dst, ALU.mult)
                last.then_inc(att_read, 1)

            def normalise(u, m):
                slot = m % 2
                dve.wait_ge(exp_done, u + 1)
                step.did(v.tensor_tensor(st[:, slot, 0, :], st[:, slot, 3, :], st[:, slot, 4, :], ALU.add))
                step.settle()
                step.did(v.reciprocal(st[:, slot, 5, :], st[:, slot, 0, :]))
                step.settle()
                for g in range(G):
                    last = v.tensor_scalar(prob[:, slot, g, :], prob[:, slot, g, :], st[:, slot, 5, g:g + 1],
                                           None, ALU.mult)
                last.then_inc(prob_done, 1)

            def attention_half(i, m, first=False):
                u = i * 8 + m
                if not first or m >= 2:
                    tok = bass.ds(i * (2 * P) + ((m - 2) // 4) * P, P)
                    gate_output(u - 2, (m - 2) % 8, tok)
                mask_scores(u, m, 1 if m >= 4 else (0 if first else 2), first and m == 0)
                if not first or m >= 1:
                    split_probs(u - 1, (m - 1) % 8)
                normalise(u, m)

            for m in range(8):
                attention_half(0, m, first=True)
            with dve.Fori(1, PBLK // 2) as i:
                step.loop(i, 1, 16)
                for m in range(8):
                    attention_half(i, m)
            step.leave(PBLK // 2 - 1, 16)
            end, last_tok = PBLK * NKV, slice(SEQ - P, SEQ)
            gate_output(end - 2, 6, last_tok)
            split_probs(end - 1, 7)
            gate_output(end - 1, 7, last_tok)
            dve.wait_ge(att_read, ATT_ROUNDS)

            ends = (slice(HIST, HIST + SEQ), slice(HIST + SEQ, UL))
            for g in range(4):
                w = 2 << g
                for h in range(2):
                    tile_free(dve, POOL_TILE + 6 * g + h)
                    ge(dve, r_ready, 2 * g + h)
                    src, dst, d = ub[:, h, :], wa[:], 1
                    while d < w:
                        step.did(v.tensor_tensor(dst[:, 2 * d - 1:], src[:, 2 * d - 1:], src[:, d - 1:UL - d], ALU.add))
                        step.settle()
                        src, dst, d = dst, (wb[:] if d in (1, 4) else wa[:]), 2 * d
                    r = dst[:, 0:T]
                    v.scalar_tensor_tensor(r[:, 0:SEQ], src[:, HIST:HIST + SEQ], 1.0 / w, ub[:, h, HIST:HIST + SEQ],
                                           ALU.mult, ALU.subtract)
                    step.did(v.scalar_tensor_tensor(
                        r[:, SEQ:T].rearrange("p (b n) -> p b n", n=NT),
                        src[:, HIST + SEQ:UL].rearrange("p (b n) -> p b n", n=SEG)[:, :, HIST:SEG], 1.0 / w,
                        ub[:, h, HIST + SEQ:UL].rearrange("p (b n) -> p b n", n=SEG)[:, :, HIST:SEG],
                        ALU.mult, ALU.subtract))
                    step.settle()
                    step.did(v.tensor_tensor(r[:, 0:w - 1], src[:, HIST:HIST + w - 1], rcv[:, 0:w - 1], ALU.mult))
                    step.settle()
                    step.did(v.tensor_tensor(r[:, 0:w - 1], r[:, 0:w - 1], ub[:, h, HIST:HIST + w - 1], ALU.subtract))
                    step.settle()
                    ge(dve, tile_done, POOL_TILE + 6 * g)
                    step.did(v.tensor_copy(r_hi[:, h, :], r))
                    step.settle()
                    v.tensor_tensor(r_lo[:, h, :], r, r_hi32[:, h, :], ALU.subtract).then_inc(r_ready, 1)
                for h in range(2):
                    n = POOL_TILE + 6 * g + 4 + h
                    k = 2 * g + h
                    dve.wait_ge(tile_done, n + 1)
                    tile_free(dve, n - 2)
                    if g == 0 and h == 0:
                        dve.wait_ge(yb_stored, 16)
                    v.scalar_tensor_tensor(thirds(sa[:, k, :]), pset(n), ps8[:, k:k + 1], thirds(zs[:, h, :]),
                                           ALU.mult, ALU.mult).then_inc(set_free[h], 1)
                    if g == 3:
                        for kk in (range(7) if h == 0 else range(7, 8)):
                            split_lo(kk, KT + kk + 1)

            dve.wait_ge(pool_stored, 16 * 2 * KT)

            def gated(base, m, j, par, second):
                dve.wait_ge(tile_done, j + (base + 1))
                dve.wait_ge(gin_loaded[par], m)
                out = mix[:, j, :] if isinstance(j, int) else mix[:, bass.ds(j, 1), :].rearrange("p a n -> p (a n)")
                if not second:
                    v.tensor_tensor(thirds(out), pset(par), thirds(gin[:, par, :]), ALU.mult)\
                        .then_inc(set_free[par], 1)
                else:
                    if not (isinstance(j, int) and j == 0):
                        step.settle()
                    v.tensor_tensor(thirds(gtmp[:]), pset(par), thirds(gin[:, par, :]), ALU.mult)\
                        .then_inc(set_free[par], 1)
                    dve.wait_ge(set_free[par], half_of(base, j, par) + 1)
                    step.did(v.tensor_tensor(out, out, gtmp[:], ALU.add))

            def half_of(base, j, par):
                return halves[0] + base // 2

            halves = [0]

            def stage(base, loads, second):
                with dve.Fori(0, 3) as i:
                    if second:
                        step.loop(i, 0, 2)
                    halves[0] = i
                    for h in range(2):
                        gated(base, (i + loads) * 16 + 16, i * 2 + h, h, second)
                if second:
                    step.leave(3, 2)
                halves[0] = 3

            stage(PP_TILE, 0, False)
            gated(PP_TILE, 64, 6, 0, False)
            for k in range(7):
                split_lo(k, 2 * KT + k + 1)
            gated(PP_TILE, 64, 7, 1, False)
            split_lo(7, 3 * KT)

            stage(PA_TILE, 4, True)
            gated(PA_TILE, 128, 6, 0, True)
            step.settle()

            def split_mix(k):
                dve.wait_ge(m_hi_done, 3 * KT + k + 1)
                v.tensor_tensor(m_lo[:, k, :], mix[:, k, :], m_hi32[:, k, :], ALU.subtract).then_inc(m_ready, 1)

            v.memset(gtmp[:, 0:1], 0.0).then_inc(mix_ready, 1)
            for k in range(7):
                split_mix(k)
            gated(PA_TILE, 128, 7, 1, True)
            step.settle()
            v.memset(gtmp[:, 0:1], 0.0).then_inc(mix_ready, 1)
            split_mix(7)

            def residual(m, j, par):
                dve.wait_ge(tile_done, j + (WO_TILE + 1))
                dve.wait_ge(gin_loaded[par], m)
                out = sa[:, j, :] if isinstance(j, int) else sa[:, bass.ds(j, 1), :].rearrange("p a n -> p (a n)")
                v.tensor_tensor(thirds(out), pset(par), thirds(gin[:, par, :]), ALU.add).then_inc(set_free[par], 1)

            with dve.Fori(0, 3) as i:
                for h in range(2):
                    residual((i + 8) * 16 + 16, i * 2 + h, h)
            residual(192, 6, 0)
            for k in range(7):
                split_lo(k, 4 * KT + k + 1)
            residual(192, 7, 1)
            split_lo(7, 5 * KT)

            for k in range(2):
                for i in range(3):
                    r = 3 * k + i
                    dve.wait_ge(p_half, r + 1)
                    c0, w = 512 * i, (512 if i < 2 else NS)
                    last = v.tensor_tensor(p_lo[:, k, c0:c0 + w], ps[:, 6 + r % 2, 0:w], p_hi32[:, k, c0:c0 + w],
                                           ALU.subtract)
                    last.then_inc(p_round_free, 1)

            def final(j, par):
                n = j * 2 + (FIN_TILE + 1)
                dve.wait_ge(tile_done, n + 1)
                dve.wait_ge(set_free[0], j + (FIN_TILE // 2 + 1))
                ge(dve, y_round, (j - 1) * 3)
                dyn = not isinstance(j, int)
                hi = m_hi32[:, bass.ds(j, 1), :].rearrange("p a n -> p (a n)") if dyn else m_hi32[:, j, :]
                lo = m_lo32[:, bass.ds(j, 1), :].rearrange("p a n -> p (a n)") if dyn else m_lo32[:, j, :]
                v.tensor_tensor(thirds(yt[:, par, :]), pset(1), thirds(sg[:]), ALU.mult).then_inc(set_free[1], 1)
                dve.wait_ge(set_free[1], j + (FIN_TILE // 2 + 1))
                step.did(v.tensor_tensor(yt[:, par, :], yt[:, par, :], lo, ALU.add))
                step.settle()
                v.tensor_tensor(yt[:, par, :], yt[:, par, :], hi, ALU.add).then_inc(yt_done, 1)

            final(0, 0)
            final(1, 1)
            with dve.Fori(1, 4) as i:
                step.loop(i, 1, 2)
                for h in range(2):
                    final(i * 2 + h, h)
            step.leave(3, 2)

        @block.scalar
        def _(act):
            a = nc.scalar

            def split_hi(k, src, used=None, end=None):
                if used is not None:
                    ge(act, *((m_used, used + k + 1) if k < KT - 1 else (tile_done, end)))
                a.activation(m_hi[:, k, :], src[:, k, :], ACT.Copy).then_inc(m_hi_done, 1)

            act.wait_ge(ssq_init, 1)
            for t in range(PBLK + 1):
                w = P if t < PBLK else NS
                act.wait_ge(x_loaded[t], 16)
                ge(act, ssq_done, t)
                a.activation(saf[0:w, 2048:2048 + D], xr[0:w, t, :], ACT.Square, accum_out=rs[0:w, 0, t:t + 1])\
                    .then_inc(ssq_done, 1)
            act.wait_ge(ms_done, 1)
            a.activation(rs[:, 2, :], rs[:, 1, :], ACT.Sqrt).then_inc(std_done, 1)
            act.wait_ge(tile_done, 2)
            a.activation(hist[:].rearrange("p (a k) n -> p a (k n)", a=2), ps[:, 3:5, 0:4 * nh], ACT.Copy)\
                .then_inc(set_free[1], 1)
            for k in range(KT):
                act.wait_ge(tile_done, X_TILE + k + 1)
                ge(act, xt_stored[k % 2], 16 * (k // 2))
                a.activation(xst[:, k % 2, :], flat(k), ACT.Copy).then_inc(xt_copied, 1)
                act.wait_ge(xt_copied, k + 1)
                act.dma_start(xT_d[k], xst[:, k % 2, :]).then_inc(xt_stored[k % 2], 16)
                if k:
                    tile_free(act, X_TILE + k - 1)
                    split_hi(k - 1, sa)
            tile_free(act, X_TILE + KT - 1)
            split_hi(KT - 1, sa)

            act.wait_ge(rows_init, 1)
            for h in range(2):
                act.wait_ge(xt_stored[h], 16 * (KT // 2))
            backs = [0]

            def take(kind, j, i, r):
                act.wait_ge(round_done, r + 1)
                bank = 6 + r % 2
                if kind == "rows":
                    if i == 0:
                        ge(act, stack_done, j - 1)
                    if i < 2:
                        ins = a.activation(rows[:, j % 2, 512 * i:512 * i + 512], ps[:, bank, :], ACT.Copy)
                    else:
                        ins = a.activation(rows[0:NS, j % 2, SEQ:SEQ + P], ps[0:NS, bank, 0:P], ACT.Copy)
                    ins.then_inc(round_free, 1)
                    return
                s = 2 if kind == "q" else 4
                if i == 0:
                    ge(act, qk_stored, 16 * j)
                if i < 2 * s:
                    dst = qkst[:, i // 2, 512 * (i % 2):512 * (i % 2) + 512]
                    src = ps[:, bank, :]
                else:
                    dst = qkst[:, 0:s, SEQ:T]
                    src = ps[:, bank, 0:NS * s].rearrange("p (s n) -> p s n", n=NS)
                a.activation(dst, src, ACT.Copy).then_inc(round_free, 1)
                if i == 2 * s:
                    act.wait_ge(round_free, r + 1)
                    if kind == "q":
                        dram_dst = qT_d[2 * j:2 * j + 2].rearrange("h p n -> p h n")
                    else:
                        dram_dst = kT_d[2 * (j - 8):2 * (j - 8) + 2].rearrange("v s p n -> p (v s) n")
                    act.dma_start(dram_dst, qkst[:, 0:s, :].bitcast(F32)).then_inc(qk_stored, 16)

            def head_std(j):
                act.wait_ge(hms_done, j + 1)
                a.activation(hs[:, 2, :], hs[:, 1, :], ACT.Sqrt).then_inc(hstd_done, 1)

            def store_v(j):
                act.wait_ge(stack_done, j + 1)
                act.dma_start(v_d[:, :, 2 * (j - 10):2 * (j - 10) + 2, :].rearrange("b p v e -> p b (v e)"),
                              st32.rearrange("p (b e) -> p b e", e=512)).then_inc(v_stored, 16)

            for j in range(13):
                plan = PLAN[j]
                at = min(len(plan), 5)
                for x, (_, kind, jj, i, r) in enumerate(plan):
                    if x == at and 1 <= j <= 10:
                        head_std(j - 1)
                    take(kind, jj, i, r)
                if len(plan) <= at and 1 <= j <= 10:
                    head_std(j - 1)
                if j < 12:
                    act.wait_ge(tile_done, QKV_TILE + j + 1)
                    a.activation(thirds(sa[:, 0, :]), pset(j), ACT.Copy).then_inc(set_free[j % 2], 1)
                if j == 11:
                    store_v(10)
            store_v(11)

            def silu(i, h):
                act.wait_ge(tile_done, i * 4 + (GATE_TILE + h + 1))
                out = sa[:, bass.ds(i * 4 + h, 1), :].rearrange("p a n -> p (a n)")
                a.activation(thirds(out), pset(h), ACT.Silu).then_inc(set_free[h % 2], 1)

            act.wait_ge(v_stored, 32)
            with act.Fori(0, 2) as i:
                for g in range(2):
                    kv = i * 2 + g
                    act.wait_ge(samp_out, kv + 1)
                    for part, q in ((0, q_even), (1, q_odd)):
                        a.activation(q_group[:, part, :], q[:, bass.ds(kv * P, P)], ACT.Copy)
                    act.wait_ge(samp_done, kv * 8 + 1)
                    a.activation(kts[:], ps[:, 6, :], ACT.Copy).then_inc(key_copied, 1)
                    silu(i, 2 * g)
                    act.wait_ge(s_shift, kv + 1)
                    a.activation(sprob[:], sprob[:], ACT.Exp, bias=sst[:, 1:2], accum_out=sst[:, 3:4])
                    a.activation(sst[:, 4:5], sst[:, 2:3], ACT.Exp).then_inc(s_exp, 1)
                    act.wait_ge(v_new_loaded, 16)
                    a.activation(v_group[0:NS, :], v_new[0:NS, bass.ds(kv, 1), :].rearrange("p a e -> p (a e)"), ACT.Copy)
                    for r, (bank, rows_, w) in enumerate(((6, P, 4), (7, P, 4), (6, NS, 1))):
                        act.wait_ge(samp_done, kv * 8 + (5 + r))
                        a.activation(spt[0:rows_, 4 * r:4 * r + w, :],
                                     ps[0:rows_, bank, 0:P * w].rearrange("p (b n) -> p b n", n=P), ACT.Copy)\
                            .then_inc(spt_copied, 1)
                    silu(i, 2 * g + 1)

            act.wait_ge(zero_done, 2)

            def gate(m, h, before):
                act.wait_ge(tile_done, m + (GATE_TILE + KT + 1))
                if before is not None:
                    act.wait_ge(gate_stored[h], before * 16)
                a.activation(thirds(gst[:, h, :]), pset(h), ACT.Sigmoid).then_inc(set_free[h], 1)
                act.wait_ge(set_free[h], gate_half[0] + (GATE_TILE + KT) // 2 + 1)
                act.dma_start(gate_d[m], gst[:, h, :]).then_inc(gate_stored[h], 16)

            gate_half = [0]

            def hi_probs(u):
                for s in range(2):
                    act.wait_ge(att_done, att_round("T", u) + s + 1)
                    bank = 6 + (att_bank("T", u_slot[0]) + s) % 2
                    a.activation(pt_hi[:, s, :], ps[:, bank, :], ACT.Copy).then_inc(pt_hi_done, 1)

            u_slot = [0]

            def exps(u, m):
                slot = m % 2
                act.wait_ge(shift_done, u + 1)
                for g in range(G):
                    a.activation(prob[:, slot, g, :], prob[:, slot, g, :], ACT.Exp, bias=st[:, slot, 1, g:g + 1],
                                 accum_out=st[:, slot, 3, g:g + 1])
                a.activation(st[:, slot, 4, :], st[:, slot, 2, :], ACT.Exp).then_inc(exp_done, 1)

            def attention_tiles(i, first=False):
                for m in range(8):
                    u = i * 8 + m
                    if not first or m >= 1:
                        u_slot[0] = (m - 1) % 8
                        hi_probs(u - 1)
                    exps(u, m)
                    if m % 2:
                        h = m // 2
                        gate_half[0] = i * 2 + h // 2
                        gate(i * 4 + h, h % 2, None if first and h < 2 else i * 2 + h // 2)

            attention_tiles(0, first=True)
            with act.Fori(1, PBLK // 2) as i:
                attention_tiles(i)
            u_slot[0] = 7
            hi_probs(PBLK * NKV - 1)

            act.wait_ge(att_read, ATT_ROUNDS)
            for h in range(2):
                act.wait_ge(gate_stored[h], 16 * KT)
            a.memzero(ub[:, :, 0:HIST]).then_inc(pool_copied, 1)
            act.wait_ge(pool_copied, 1)

            def take_history(k, need):
                act.wait_ge(pool_t, need)
                ge(act, pool_stored, 32 * (k))
                a.activation(pst[0:nh, 0, :], ps[0:nh, 6, 0:P], ACT.Copy)
                a.activation(pst[0:HIST, 1, :], ps[0:HIST, 6, P:2 * P], ACT.Copy).then_inc(pool_copied, 1)
                act.wait_ge(pool_copied, need + 1)
                cols = bass.ds(k * P, P)
                act.dma_start(npool_s[:, cols], pst[0:nh, 0, :]).then_inc(pool_stored, 16)
                act.dma_start(npool_p[:, cols], pst[0:HIST, 1, :]).then_inc(pool_stored, 16)

            def pool_group(g, first=False):
                for h in range(2):
                    k = g * 2 + h
                    act.wait_ge(tile_done, g * 6 + (POOL_TILE + h + 1))
                    if not first:
                        act.wait_ge(r_ready, g * 2 + (h - 1))
                    sam = ub[:, h, HIST + SEQ:UL].rearrange("p (b n) -> p b n", n=SEG)
                    old = hist[:, k, :] if first else hist[:, bass.ds(k, 1), :].rearrange("p a n -> p (a n)")
                    a.activation(sam[:, :, 0:HIST], old.rearrange("p (b n) -> p b n", n=HIST), ACT.Copy)
                    a.activation(ub[:, h, HIST:HIST + 2 * CH].rearrange("p (c n) -> p c n", n=CH),
                                 ps[:, 3 * h:3 * h + 2, 0:CH], ACT.Copy)
                    a.activation(ub[:, h, HIST + 2 * CH:HIST + SEQ], ps[:, 3 * h + 2, 0:SEQ - 2 * CH], ACT.Copy)
                    a.activation(sam[:, :, HIST:SEG],
                                 ps[:, 3 * h + 2, SEQ - 2 * CH:CH].rearrange("p (b n) -> p b n", n=NT), ACT.Copy)\
                        .then_inc(set_free[h], 1)
                    act.wait_ge(set_free[h], g * 3 + (POOL_TILE // 2 + 1))
                    a.activation(keep[:, h, :].rearrange("p (b n) -> p b n", n=HIST), sam[:, :, NT:SEG], ACT.Copy)\
                        .then_inc(keep_ready, 1)
                for h in range(2):
                    k = g * 2 + h
                    act.wait_ge(tile_done, g * 6 + (POOL_TILE + 2 + h + 1))
                    a.activation(thirds(zs[:, h, :]), pset(h), ACT.Silu).then_inc(set_free[h], 1)
                    take_history(k, k + 1)

            pool_group(0, first=True)
            with act.Fori(1, 3) as g:
                pool_group(g)
            pool_group(3)
            for k in range(KT):
                tile_free(act, POOL_TILE + 22 + k // 7) if k in (0, 7) else None
                split_hi(k, sa, 3 * (KT - 1), POOL_TILE + 22)
            act.wait_ge(yb_loaded, 16)
            for k in range(KT):
                split_hi(k, sa, 5 * (KT - 1), PA_TILE)
            for k in range(KT):
                ge(act, mix_ready, 1 if k < 7 else 2)
                split_hi(k, mix, 7 * (KT - 1), WO_TILE)
            for k in range(KT):
                tile_free(act, WO_TILE + 6 + k // 7) if k in (0, 7) else None
                split_hi(k, sa, 9 * (KT - 1), FIN_TILE)

            for r in range(6):
                k, i = divmod(r, 3)
                c0, w = 512 * i, (512 if i < 2 else NS)
                act.wait_ge(p_round, r + 1)
                a.activation(p_hi[:, k, c0:c0 + w], ps[:, 6 + r % 2, 0:w], ACT.Copy).then_inc(p_half, 1)

            def take_y(c, h, r, i):
                act.wait_ge(y_round, r + 1)
                bank = 6 + (3 * h + i) % 2
                if i < 2:
                    a.activation(yrow[:, 4 * i:4 * i + 4, P * h:P * h + P],
                                 ps[:, bank, :].rearrange("p (b n) -> p b n", n=P), ACT.Copy).then_inc(y_round_free, 1)
                else:
                    a.activation(yrow[0:NS, PBLK, P * h:P * h + P], ps[0:NS, bank, 0:P], ACT.Copy)\
                        .then_inc(y_round_free, 1)

            def take_tile(c, h, j):
                if h == 0:
                    ge(act, y_stored, c * 32)
                for i in range(3):
                    take_y(c, h, j * 3 + i, i)
                if h == 1:
                    act.wait_ge(y_round_free, j * 3 + 3)
                    cols = bass.ds(c * WC, WC)
                    act.dma_start(y_p[:, cols].rearrange("(b p) n -> p b n", p=P), yrow[:, 0:PBLK, :])\
                        .then_inc(y_stored, 16)
                    act.dma_start(y_s[:, cols], yrow[0:NS, PBLK, :]).then_inc(y_stored, 16)

            def final(j):
                act.wait_ge(tile_done, j * 2 + (FIN_TILE + 1))
                ge(act, set_free[1], j + FIN_TILE // 2)
                a.activation(thirds(sg[:]), pset(0), ACT.Sigmoid).then_inc(set_free[0], 1)

            final(0)
            take_tile(0, 0, 0)
            final(1)
            with act.Fori(1, 4) as c:
                take_tile(c - 1, 1, c * 2 - 1)
                final(c * 2)
                take_tile(c, 0, c * 2)
                final(c * 2 + 1)
            take_tile(3, 1, 7)
            act.wait_ge(y_stored, 32 * 4)
            act.wait_ge(pool_stored, 32 * KT)


def plan_rounds():
    plan, r = [], 0
    rows_end, back_end = [0] * 12, [0] * 12
    for j in range(13):
        here = []
        if j:
            for i in range(3):
                here.append((1 + i, "rows", j - 1, i, r))
                r += 1
            rows_end[j - 1] = r
        if 2 <= j <= 11:
            kind, count = ("q", 5) if j - 2 < 8 else ("k", 9)
            for i in range(count):
                here.append((4 + i * 3 // count, kind, j - 2, i, r))
                r += 1
            back_end[j - 2] = r
        plan.append(here)
    return plan, rows_end, back_end, r


PLAN, ROWS_END, BACK_END, ROUNDS = plan_rounds()

_IN = (("x_prompt", (SEQ, D)), ("x_sample", (NS, D)), ("cache_k", (NB, P, NKV * HD)), ("cache_v", (NB, P, NKV * HD)),
       ("state_pool", (NB * HIST, D)), ("p_prompt", (SEQ, PLE)), ("p_sample", (NS, PLE)), ("params", None),
       ("w_in", (D, 6656)), ("pool_map", (4, 256, 256)), ("w_proj_pool", (D, D)), ("w_proj_attn", (D, D)),
       ("w_out", (D, D)), ("w_ple", (PLE, D)), ("w_ple_gate", (D, D)), ("const", None), ("masks", None),
       ("smask", None))
_OUT = (("y_p", (SEQ, D)), ("y_s", (NS, D)), ("nk_p", (P, 256)), ("nv_p", (P, 256)), ("npool_p", (HIST, D)),
        ("nk_s", (NB, P, 256)), ("nv_s", (NB, P, 256)), ("npool_s", (NB * HIST, D)))


def kernel(**inputs):
    import concourse.bacc as bacc
    from concourse.bass_utils import run_bass_kernel_spmd

    x = {k: np.asarray(v) for k, v in inputs.items()}
    cols = [x["norm_g"].reshape(8, P).T, x["pool_scale"].reshape(8, P).T]
    for name in ("q_norm_g", "k_norm_g", "sinks"):
        cols.append(np.broadcast_to(x[name].reshape(1, -1), (P, x[name].size)))
    cols.append(np.repeat(x["sinks"].reshape(NKV, G).T, NS, axis=0))
    x["params"] = np.concatenate(cols, axis=1)
    x["const"], x["masks"], x["smask"] = consts()
    nc = bacc.Bacc("TRN2", target_bir_lowering=False, num_devices=1)
    arrays, args = {}, []
    for name, shape in _IN:
        arr = np.ascontiguousarray(x[name] if shape is None else x[name].reshape(shape))
        arrays[f"in_{name}"] = arr
        args.append(nc.dram_tensor(f"in_{name}", arr.shape, mybir.dt.from_np(arr.dtype), kind="ExternalInput").ap())
    for name, shape in _OUT:
        args.append(nc.dram_tensor(f"out_{name}", shape, F32, kind="ExternalOutput").ap())
    build(nc, *args)
    r = run_bass_kernel_spmd(nc, [arrays], core_ids=[0]).results[0]
    o = {name: r[f"out_{name}"] for name, _ in _OUT}
    return (o["y_p"].reshape(1, SEQ, D), o["y_s"].reshape(NB, NT, D), o["nk_p"].reshape(1, 1, P, NKV, HD),
            o["nv_p"].reshape(1, 1, P, NKV, HD), o["npool_p"].reshape(1, 1, HIST, D),
            o["nk_s"].reshape(1, NB, P, NKV, HD), o["nv_s"].reshape(1, NB, P, NKV, HD),
            o["npool_s"].reshape(1, NB, HIST, D))
```

```python
from contextlib import ExitStack

import numpy as np

import concourse.bass as bass
from concourse import mybir

F32 = mybir.dt.float32
F32R = mybir.dt.float32r
ALU = mybir.AluOpType
ACT = mybir.ActivationFunctionType
AX_X = mybir.AxisListType.X

P = 128
D = 1024
KT = D // P
SEQ, NB, NT = 1024, 8, 4
NS = NB * NT
T = SEQ + NS
NCH = 3
CH = T // NCH
PBLK = SEQ // P
HD, NH, NKV, G = 64, 16, 4, 4
HIST = 15
SEG = HIST + NT
UL = HIST + SEQ + NB * SEG
PLE = 256
EPS = 1e-6
NEG = -3.0e38
WC = 256
XKT = 2
SEQ_ORDER = (0, 2, 4, 6, 1, 3, 5, 7)
COL = dict(u=0, zp=D, q=2 * D, k=3 * D, v=3 * D + 256, za=3 * D + 512, ga=4 * D + 512, gb=5 * D + 512)

QKV_TILE = 2
GATE_TILE = QKV_TILE + 12
POOL_TILE = GATE_TILE + 24
PP_TILE = POOL_TILE + 24
PA_TILE = PP_TILE + 8
WO_TILE = PA_TILE + 8
FIN_TILE = WO_TILE + 8
QKV_CHUNK, GATE_CHUNK, POOL_CHUNK, PP_CHUNK, PA_CHUNK, WO_CHUNK, FIN_CHUNK = 0, 6, 18, 26, 30, 34, 38


def chunk_end(n):
    if n < GATE_CHUNK:
        return QKV_TILE + 2 * (n + 1)
    if n < POOL_CHUNK:
        return GATE_TILE + 2 * (n - GATE_CHUNK + 1)
    if n < PP_CHUNK:
        g, second = divmod(n - POOL_CHUNK, 2)
        return POOL_TILE + 6 * g + (6 if second else 2)
    if n < FIN_CHUNK:
        return PP_TILE + 2 * (n - PP_CHUNK + 1)
    return FIN_TILE + 4 * (n - FIN_CHUNK + 1)


def ge(eng, sem, value):
    if not isinstance(value, int) or value > 0:
        eng.wait_ge(sem, value)


class Steps:

    def __init__(self, eng, sem):
        self.eng, self.sem, self.n = eng, sem, 0

    def did(self, ins):
        ins.then_inc(self.sem, 1)
        self.n = self.n + 1

    def settle(self):
        ge(self.eng, self.sem, self.n)

    def loop(self, i, first, per):
        self.base = self.n
        self.n = (i - first) * per + self.base

    def leave(self, count, per):
        self.n = self.base + count * per


def att_round(kind, u):
    if kind == "S":
        return 0 if isinstance(u, int) and u == 0 else u * 5 - 3
    if kind == "T":
        last = isinstance(u, int) and u == PBLK * NKV - 1
        return u * 5 + (2 if last else 4)
    return u * 5 + (4 if isinstance(u, int) and u == PBLK * NKV - 1 else 6)


ATT_ROUNDS = 5 * PBLK * NKV


def att_bank(kind, m, first=False):
    if first:
        return 6
    return 6 + {"S": m + 1, "T": m, "V": m}[kind] % 2


X_BANK = [(6, 1)[t % 2] for t in range(PBLK)] + [0]
RMS_GROUPS = ((0, PBLK // 2 + 1), (PBLK // 2 + 1, PBLK + 1))


def consts():
    j = np.arange(P)
    cur = np.where(j[None, :] <= j[:, None], 0.0, NEG)
    prev = np.where(j[None, :] >= j[:, None], 0.0, NEG)
    none = np.full((P, P), NEG)
    masks = np.stack([np.concatenate(x, 1) for x in ((cur, none), (prev, cur), (cur, prev))], 1)
    row = np.arange(P)
    b, t = (row % NS) // NT, row % NT
    smask = np.full((P, NB + 1, P), NEG)
    for at, seq in enumerate(SEQ_ORDER):
        smask[:, at] = np.where((b[:, None] == seq) & (j[None, :] >= t[:, None]), 0.0, NEG)
    n = np.arange(NS)
    smask[:, NB, :NS] = np.where((b[:, None] == n[None, :] // NT) & (n[None, :] % NT <= t[:, None]), 0.0, NEG)
    smask = smask.reshape(P, -1)[:, :T]
    inv = (np.float32(500000.0) ** (-np.arange(0, 16, 2, dtype=np.float32) / np.float32(16))).astype(np.float32)
    pos = (np.arange(PBLK + 1)[None, :] * P + j[:, None]).astype(np.float32)
    pos[:, PBLK] = 2048 + j % NT
    ang = (pos[:, :, None] * inv).astype(np.float32).astype(np.float64)
    ang = np.repeat(ang, 2, axis=1)
    rc = np.broadcast_to(1.0 / (np.arange(HIST) + 1.0), (P, HIST))
    parts = (np.eye(P), np.cos(ang).reshape(P, -1), np.sin(ang).reshape(P, -1), rc)
    small = np.concatenate(parts, 1)
    return (np.ascontiguousarray(small, np.float32), np.ascontiguousarray(masks.reshape(P, -1), np.float32),
            np.ascontiguousarray(smask, np.float32))


CONST_W = P + 2 * 18 * 8 + HIST
PARAM_W = 8 + 8 + 64 + 64 + 16 + 4


def build(nc, xp, xs, cache_k, cache_v, state, pp, ps_, params, w_in, pool_map, w_pp, w_pa, w_out, w_ple,
          w_gate, const, masks, smask, y_p, y_s, nk_p, nv_p, npool_p, nk_s, nv_s, npool_s):
    with ExitStack() as ctx:
        def sb(name, shape, dt=F32, scope=ctx):
            return scope.enter_context(nc.sbuf_tensor(name, shape, dt))

        def sem(name):
            return ctx.enter_context(nc.semaphore(name))

        def dram(name, shape, dt=F32):
            return nc.dram_tensor(name, shape, dt, kind="Internal").ap()

        xT_d = dram("xT_d", (KT, P, T))
        gate_d = dram("gate_d", (2 * KT, P, T))
        yb_d = dram("yb_d", (KT, P, T))
        qk_d = dram("qk_d", (NH + NKV, P, T))
        v_d = dram("v_d", (PBLK + 1, P, NKV, P))

        m_hi, m_lo = sb("m_hi", [P, KT, T], F32R), sb("m_lo", [P, KT, T], F32R)
        sa = sb("sa", [P, KT, T])
        saf = sa[:].rearrange("p k n -> p (k n)")
        w_hi = sb("w_hi", [P, 2, KT + XKT, WC], F32R)
        w_lo = sb("w_lo", [P, 2, KT + XKT, WC], F32R)
        raw = [sb("raw_a", [P, 4, WC]), sb("raw_b", [P, 4, WC]), sb("raw_c", [P, XKT, WC])]
        par_s = sb("par_s", [P, PARAM_W])
        con_s = sb("con_s", [P, CONST_W])
        hist = sb("hist", [P, KT, NB * HIST])
        w_one = sb("w_one", [P, 1])
        warm = sb("warm", [P, 2])
        kv_out = sb("kv_out", [P, 2, 2 * NKV * HD])
        g8, ps8, qg, kg, sinks, sinks_s = (par_s[:, a:b] for a, b in
                                          ((0, 8), (8, 16), (16, 80), (80, 144), (144, 160), (160, 164)))
        ident = con_s[:, 0:P]
        cosv = con_s[:, P:P + 144].rearrange("p (a c) -> p a c", c=8)
        sinv = con_s[:, P + 144:P + 288].rearrange("p (a c) -> p a c", c=8)
        rcv = con_s[:, P + 288:P + 288 + HIST]

        with ExitStack() as s0:
            xr = sb("xr", [P, PBLK + 1, D], scope=s0)
            rbc = sb("rbc", [P, T], scope=s0)
            xn = sb("xn", [P, 2, T], scope=s0)
            rs = sb("rs", [P, 4, PBLK + 1], scope=s0)
        with ExitStack() as s1:
            qkst = sb("qkst", [P, 2, T], F32R, scope=s1)
            stack = sb("stack", [P, 2, (PBLK + 1) * 256], F32R, scope=s1)
            hs = sb("hs", [P, 4, 18], scope=s1)
        with ExitStack() as s4:
            spt = sb("spt", [P, NB + 1, P], scope=s4)
            vc = sb("vc", [P, 2, NB, 2, HD], scope=s4)
            v_new = sb("v_new", [P, NKV, P], scope=s4)
            v_group = sb("v_group", [P, 2, 2, HD], scope=s4)
            s_out = sb("s_out", [P, KT, NS], scope=s4)
            sb("s_gap", [P, 2592], scope=s4)
            kc = sb("kc", [P, 2, NB, HD], scope=s4)
            kts = sb("kts", [P, NB // 2 * P], scope=s4)
            q_sum, q_low = (sb(n, [P, (NH + NKV) * NS], scope=s4) for n in ("q_sum", "q_low"))
            smsk = sb("smsk", [P, T], scope=s4)
            q_group = sb("q_group", [P, 2, P], scope=s4)
            sst = sb("sst", [P, 8], scope=s4)
            sprob = sb("sprob", [P, T], scope=s4)
        with ExitStack() as s3:
            vt = sb("vt", [P, 2, NKV, 2 * P], F32R, scope=s3)
            prob = sb("prob", [P, 2, G, 2 * P], scope=s3)
            gst = sb("gst", [P, 2, T], scope=s3)
            pt_hi = [sb("pt_hi0", [P, G * P], F32R, scope=s3)]
            sb("p_gap", [P, 80], scope=s3)
            qt = sb("qt", [P, 2, G, P], F32R, scope=s3)
            kt = sb("kt", [P, NKV, 2, 2, P], F32R, scope=s3)
            msk = sb("msk", [P, 3, 2 * P], scope=s3)
            pt_hi.append(sb("pt_hi1", [P, G * P], F32R, scope=s3))
            pt_lo = [sb(f"pt_lo{i}", [P, G * P], F32R, scope=s3) for i in range(2)]
            st = sb("st", [P, 2, 6, G], scope=s3)
        with ExitStack() as s5:
            ub = sb("ub", [P, 2, UL], scope=s5)
            wa, wb = sb("wa", [P, UL], scope=s5), sb("wb", [P, UL], scope=s5)
            r_hi, r_lo = sb("r_hi", [P, 2, T], F32R, scope=s5), sb("r_lo", [P, 2, T], F32R, scope=s5)
            zs = sb("zs", [P, 2, T], scope=s5)
            keep = sb("keep", [P, 2, NB * HIST], scope=s5)
            pst = sb("pst", [P, 2, P], scope=s5)
        gin = sb("gin", [P, 2, T])
        with ExitStack() as s6:
            mix = sb("mix", [P, KT, T], scope=s6)
            gtmp = sb("gtmp", [P, T], scope=s6)
        with ExitStack() as s7:
            p_hi, p_lo = sb("p_hi", [P, 2, T], F32R, scope=s7), sb("p_lo", [P, 2, T], F32R, scope=s7)
            yrow = sb("yrow", [P, PBLK + 1, WC], scope=s7)
            sg = sb("sg", [P, T], scope=s7)
            yt = sb("yt", [P, 2, T], scope=s7)

        ps = ctx.enter_context(nc.psum_tensor("ps", [P, 8, 512], F32))
        psf = ps[:].rearrange("p b n -> p (b n)")

        def pset(n):
            return ps[:, 3 * (n % 2):3 * (n % 2) + 3, 0:CH]

        def flat(n, w=T):
            return psf[:, 1536 * (n % 2):1536 * (n % 2) + w]

        def thirds(ap):
            return ap.rearrange("p (c n) -> p c n", c=NCH)

        par_loaded, con_loaded, hist_loaded = sem("par_loaded"), sem("con_loaded"), sem("hist_loaded")
        x_loaded = [sem(f"x_loaded{t}") for t in range(PBLK + 1)]
        raw_loaded = [sem(f"raw_loaded{i}") for i in range(3)]
        raw_hi = sem("raw_hi")
        piece_split = [sem(f"piece_split{i}") for i in range(3)]
        tile_done = sem("tile_done")
        set_free = [sem("set_free0"), sem("set_free1")]
        m_used = sem("m_used")
        m_hi_done, m_ready = sem("m_hi_done"), sem("m_ready")
        ssq_done, ms_done, std_done, rms_done, rms_spread = (
            sem("ssq_done"), sem("ms_done"), sem("std_done"), sem("rms_done"), sem("rms_spread"))
        xb_done, xb_copied, xn_done, xt_stored = sem("xb_done"), sem("xb_copied"), sem("xn_done"), sem("xt_stored")
        hist_done, hist_copied = sem("hist_done"), sem("hist_copied")
        dve_step, warm_done = sem("dve_step"), sem("warm_done")
        round_done, round_free = sem("round_done"), sem("round_free")
        hms_done, hstd_done, stack_done = sem("hms_done"), sem("hstd_done"), sem("stack_done")
        qk_stored, v_stored, kv_kept = sem("qk_stored"), sem("v_stored"), sem("kv_kept")
        gate_stored = [sem("gate_stored0"), sem("gate_stored1")]
        samp_done, samp_out = sem("samp_done"), sem("samp_out")
        q_loaded, smask_loaded, v_new_loaded = sem("q_loaded"), sem("smask_loaded"), sem("v_new_loaded")
        kc_loaded = [sem("kc_loaded0"), sem("kc_loaded1")]
        vc_loaded = [sem("vc_loaded0"), sem("vc_loaded1")]
        key_copied, s_read, s_shift, s_exp, s_prob, spt_copied = (
            sem("key_copied"), sem("s_read"), sem("s_shift"), sem("s_exp"), sem("s_prob"), sem("spt_copied"))
        att_done, att_read = sem("att_done"), sem("att_read")
        masks_loaded, zero_done = sem("masks_loaded"), sem("zero_done")
        unit_loaded = [sem(f"unit_loaded{i}") for i in range(NKV)]
        v_loaded = [sem(f"v_loaded{i}") for i in range(NKV)]
        shift_done, exp_done, prob_done, pt_hi_done = (
            sem("shift_done"), sem("exp_done"), sem("prob_done"), sem("pt_hi_done"))
        yb_stored, yb_loaded = sem("yb_stored"), sem("yb_loaded")
        r_ready, keep_ready, pool_t, pool_copied, pool_stored = (
            sem("r_ready"), sem("keep_ready"), sem("pool_t"), sem("pool_copied"), sem("pool_stored"))
        gin_loaded = [sem("gin_loaded0"), sem("gin_loaded1")]
        p_loaded, p_round, p_round_free = sem("p_loaded"), sem("p_round"), sem("p_round_free")
        yt_done, y_round, y_round_free = sem("yt_done"), sem("y_round"), sem("y_round_free")
        y_stored = [sem("y_stored0"), sem("y_stored1")]
        out_stored = sem("out_stored")
        ssq_init, rows_init, mix_ready, p_half = (
            sem("ssq_init"), sem("rows_init"), sem("mix_ready"), sem("p_half"))

        nh = NB * HIST
        state_rows = kv_out[:].rearrange("p a n -> p (a n)")
        rows = saf[:, 2880:2880 + 2 * (PBLK + 1) * P].rearrange("p (s n) -> p s n", s=2)
        m_hi32, m_lo32 = m_hi[:].bitcast(F32), m_lo[:].bitcast(F32)
        st32 = stack[:].bitcast(F32)
        rms_rows = xn[:].rearrange("p a n -> p (a n)")[:, 0:(PBLK + 1) * P].rearrange("p (t n) -> p t n", n=P)
        k_new = q_sum[:, NH * NS:]
        r_hi32, p_hi32 = (x[:].bitcast(F32) for x in (r_hi, p_hi))

        def tile_free(eng, n):
            ge(eng, set_free[n % 2], n // 2 + 1)

        block = ctx.enter_context(nc.Block())

        @block.sync
        def _(sp):
            def load_chunk(n, w, col, extra=None, extra_n=None):
                for h in range(2):
                    ge(sp, piece_split[h], n)
                    src = w[512 * h:512 * h + 512, bass.ds(col, WC)].rearrange("(k p) n -> p k n", p=P)
                    sp.dma_start(raw[h][:], src).then_inc(raw_loaded[h], 16)
                if extra is not None:
                    ge(sp, piece_split[2], extra_n)
                    sp.dma_start(raw[2][:], extra.rearrange("(k p) n -> p k n", p=P)).then_inc(raw_loaded[2], 16)

            sp.dma_start(con_s[:], const).then_inc(con_loaded, 16)
            sp.dma_start(par_s[:], params).then_inc(par_loaded, 16)
            sp.dma_start(xr[0:NS, PBLK, :], xs).then_inc(x_loaded[PBLK], 16)
            for t in range(PBLK):
                sp.dma_start(xr[:, t, :], xp[P * t:P * t + P, :]).then_inc(x_loaded[t], 16)
            load_chunk(0, w_in, COL["q"])
            sp.wait_ge(set_free[0], 1)
            sp.wait_ge(xb_copied, PBLK)
            for k in range(0, KT, 2):
                sp.dma_start(xT_d[k:k + 2].rearrange("k p n -> p k n"), sa[:, k:k + 2, :]).then_inc(xt_stored, 16)
            sp.wait_ge(ssq_done, PBLK + 2)
            sp.dma_start(state_rows[0:NB * HIST, :], state).then_inc(hist_loaded, 16)
            with sp.Fori(1, 6) as c:
                load_chunk(c, w_in, c * WC + COL["q"])
            for b in range(NB):
                for new, old in ((nk_s, cache_k), (nv_s, cache_v)):
                    sp.dma_start(new[b, 0:P - NT, :], old[b, NT:P, :]).then_inc(out_stored, 16)
            for n in range(GATE_CHUNK, GATE_CHUNK + 2):
                load_chunk(n, w_in, (n - GATE_CHUNK) * WC + COL["za"])

            ck = cache_k.rearrange("b j (v d) -> v j b d", v=NKV)
            cv = cache_v.rearrange("b j (v d) -> v j b d", v=NKV)
            sp.dma_start(kc[:, 0], ck[0]).then_inc(kc_loaded[0], 16)
            sp.dma_start(kc[:, 1], ck[1]).then_inc(kc_loaded[1], 16)
            sp.dma_start(smsk[:], smask).then_inc(smask_loaded, 16)
            for tiles, a, b in ((8, 0, NH), (10, NH, NH + NKV)):
                sp.wait_ge(qk_stored, 16 * tiles)
                for half in range(2):
                    for part, dst in ((0, q_sum), (1, q_low)):
                        src = qk_d[a:b, HD * part:HD * part + HD, SEQ:T].rearrange("h p n -> p h n")
                        sp.dma_start(dst[HD * half:HD * half + HD, NS * a:NS * b].rearrange("p (h n) -> p h n", n=NS),
                                     src).then_inc(q_loaded, 16)
            sp.wait_ge(v_stored, 16 * 2)
            sp.dma_start(v_new[0:NS], v_d[PBLK, 0:NS]).then_inc(v_new_loaded, 16)
            for g in range(2):
                for c in range(2):
                    sp.dma_start(vc[:, g, :, c, :], cv[g]).then_inc(vc_loaded[g], 16)
            sp.wait_ge(kv_kept, 4)
            sp.dma_start(nk_p, kv_out[:, 0, 0:256]).then_inc(out_stored, 16)
            sp.dma_start(nv_p, kv_out[:, 0, 256:512]).then_inc(out_stored, 16)
            for b in range(NB):
                sp.dma_start(nk_s[b, P - NT:P, :], kv_out[NT * b:NT * b + NT, 1, 0:256]).then_inc(out_stored, 16)
                sp.dma_start(nv_s[b, P - NT:P, :], kv_out[NT * b:NT * b + NT, 1, 256:512]).then_inc(out_stored, 16)
            for g in range(2, NKV):
                load_chunk(GATE_CHUNK + g, w_in, g * WC + COL["za"])
                sp.wait_ge(key_copied, g - 1)
                sp.dma_start(kc[:, g % 2], ck[g]).then_inc(kc_loaded[g % 2], 16)
                sp.wait_ge(samp_out, g)
                for c in range(2):
                    sp.dma_start(vc[:, g % 2, :, c, :], cv[g]).then_inc(vc_loaded[g % 2], 16)
            for n in range(GATE_CHUNK + 4, GATE_CHUNK + 6):
                load_chunk(n, w_in, (n - GATE_CHUNK) * WC + COL["za"])

            def load_q_k(u, t, m):
                tok, kv = bass.ds(t * P, P), m % 4
                sp.dma_start(qt[:, m % 2, :, :].bitcast(F32),
                             qk_d[G * kv:G * kv + G, :, tok].rearrange("g p n -> p g n")).then_inc(unit_loaded[kv], 16)
                for half in range(2):
                    sp.dma_start(kt[HD * half:HD * half + HD, kv, :, m // 4, :].bitcast(F32),
                                 qk_d[NH + kv, :, tok].rearrange("(s e) n -> e s n", s=2))\
                        .then_inc(unit_loaded[kv], 16)

            def load_v(t, m):
                for c in range(2):
                    dst = vt[:, m // 4, m % 4, :].rearrange("p (s c e) -> p s c e", s=2, c=2)[:, :, c]
                    sp.dma_start(dst.bitcast(F32), v_d[t, :, m % 4, :].rearrange("p (s e) -> p s e", s=2))\
                        .then_inc(v_loaded[m % 4], 16)

            def load_unit(i, m):
                u, t = 8 * i + m, 2 * i + m // 4
                sp.wait_ge(att_done, att_round("S", u - 2) + 2)
                load_q_k(u, t, m)
                load_v(t, m)

            sp.wait_ge(s_read, 3 * NKV)
            sp.dma_start(msk[:].rearrange("p a n -> p (a n)"), masks).then_inc(masks_loaded, 16)
            for m in range(2):
                load_q_k(m, 0, m)
            sp.wait_ge(zero_done, 2)
            for m in range(2):
                load_v(0, m)

            def load_units(i, chunk_a, chunk_b):
                for m in range(2, 8):
                    load_unit(i, m)
                    if m == 2:
                        load_chunk(*chunk_a)
                    if m == 6:
                        load_chunk(*chunk_b)

            def gate_chunk(n):
                return n, w_in, (n - GATE_CHUNK) * WC + COL["za"]

            load_units(0, gate_chunk(GATE_CHUNK + 6), gate_chunk(GATE_CHUNK + 7))
            with sp.Fori(1, 3) as i:
                for m in range(2):
                    load_unit(i, m)
                load_units(i, gate_chunk(i * 2 + (GATE_CHUNK + 6)), gate_chunk(i * 2 + (GATE_CHUNK + 7)))
            for m in range(2):
                load_unit(3, m)
            load_units(3, (POOL_CHUNK, w_in, 0), (POOL_CHUNK + 1, w_in, COL["zp"], pool_map[0], 0))
            sp.wait_ge(att_read, ATT_ROUNDS)
            sp.dma_start(yb_d.rearrange("k p n -> p k n"), sa[:]).then_inc(yb_stored, 16)

            with sp.Fori(1, 4) as g:
                load_chunk(g * 2 + POOL_CHUNK, w_in, g * WC)
                load_chunk(g * 2 + POOL_CHUNK + 1, w_in, g * WC + COL["zp"], pool_map[g], g)

            def stage(base, chunk, w, src, early=None):
                def turn(c, chunk_too=True):
                    if chunk_too:
                        load_chunk(c + chunk, w, c * WC)
                    for h in range(2):
                        sp.wait_ge(set_free[h], c + base // 2)
                        sp.dma_start(gin[:, h, :], src[c * 2 + h]).then_inc(gin_loaded[h], 16)

                turn(0)
                load_chunk(chunk + 1, w, WC)
                if early is not None:
                    early()
                turn(1, False)
                with sp.Fori(2, 4) as c:
                    turn(c)

            def load_yb():
                sp.wait_ge(m_ready, 2 * KT)
                sp.wait_ge(yb_stored, 16)
                sp.dma_start(sa[:], yb_d.rearrange("k p n -> p k n")).then_inc(yb_loaded, 16)

            def load_p():
                sp.wait_ge(m_ready, 4 * KT)
                for t in range(PBLK):
                    sp.dma_start(yrow[:, t, :], pp[P * t:P * t + P, :]).then_inc(p_loaded, 16)
                sp.dma_start(yrow[0:NS, PBLK, :], ps_).then_inc(p_loaded, 16)

            stage(PP_TILE, PP_CHUNK, w_pp, gate_d, load_yb)
            stage(PA_TILE, PA_CHUNK, w_pa, gate_d[KT:2 * KT])
            sp.wait_ge(xt_stored, 16 * (KT // 2))
            stage(WO_TILE, WO_CHUNK, w_out, xT_d, load_p)
            load_chunk(FIN_CHUNK, w_gate, 0, w_ple[:, 0:WC], 4)
            with sp.Fori(1, 4) as c:
                load_chunk(c + FIN_CHUNK, w_gate, c * WC, w_ple[:, bass.ds(c * WC, WC)], c + 4)
            sp.wait_ge(out_stored, 16 * (2 * NB + 2 + 2 * NB))

        @block.gpsimd
        def _(pool):
            hi_count = Steps(pool, raw_hi)
            hi_count.did(nc.gpsimd.memset(w_one[:], 1.0))
            hi_count.settle()

            def split(n, slot, end, piece, k0, kn, m):
                pool.wait_ge(raw_loaded[piece], (m + 1) * 16)
                ge(pool, tile_done, end)
                hi, lo = w_hi[:, slot, k0:k0 + kn, :], w_lo[:, slot, k0:k0 + kn, :]
                one = w_one[:, 0:1].unsqueeze(2).to_broadcast([P, kn, WC])
                hi_count.did(nc.gpsimd.tensor_tensor(hi, raw[piece][:], one, ALU.mult))
                hi_count.settle()
                nc.gpsimd.tensor_tensor(lo, raw[piece][:], hi.bitcast(F32), ALU.subtract)\
                    .then_inc(piece_split[piece], 1)

            def chunk(n, slot, end, m=None):
                split(n, slot, end, 0, 0, 4, n)
                split(n, slot, end, 1, 4, 4, n)
                if m is not None:
                    split(n, slot, end, 2, KT, XKT, m)

            def chunks(first, count, per_pair, steps, extra=None):
                for h in range(2):
                    n = first + h
                    chunk(n, h, chunk_end(n - 2) if n >= 2 else 0, extra(0, h) if extra else None)
                with pool.Fori(1, count // 2) as i:
                    hi_count.loop(i, 1, steps)
                    for h in range(2):
                        done = i * per_pair + (chunk_end(first + h) - per_pair)
                        chunk(i * 2 + (first + h), h, done, extra(i, h) if extra else None)
                hi_count.leave(count // 2 - 1, steps)

            chunks(QKV_CHUNK, 6, 4, 4)
            chunks(GATE_CHUNK, 12, 4, 4)
            chunks(POOL_CHUNK, 8, 6, 5, lambda i, h: i if h else None)
            chunks(PP_CHUNK, 4, 4, 4)
            chunks(PA_CHUNK, 4, 4, 4)
            chunks(WO_CHUNK, 4, 4, 4)
            chunks(FIN_CHUNK, 4, 8, 6, lambda i, h: i * 2 + (4 + h))

        @block.tensor
        def _(pe):
            def project(parity, free, slot, f, src_hi, src_lo, wait_m=None, used=False, k0=0, kn=KT,
                        pieces=None, after=None, done=False):
                ge(pe, set_free[parity], free)
                for k in range(kn):
                    for at, sem_, value in pieces or ():
                        if at == k:
                            pe.wait_ge(sem_, value)
                    if wait_m is not None:
                        pe.wait_ge(m_ready, wait_m + (k + 1))
                    last = products(parity, slot, f, src_hi, src_lo, k, k0, kn)
                    if used and k < kn - 1:
                        last.then_inc(m_used, 1)
                    if done and k == kn - 1:
                        last.then_inc(tile_done, 1)
                    for call in (after or {}).get(k, ()):
                        call()
                return last

            def products(parity, slot, f, src_hi, src_lo, k, k0=0, kn=KT):
                wh = w_hi[:, slot, k0 + k, P * f:P * f + P]
                wl = w_lo[:, slot, k0 + k, P * f:P * f + P]
                for w, parts in ((wh, (src_hi, src_lo)), (wl, (src_hi,))):
                    for c in range(NCH):
                        for x in parts:
                            last = nc.tensor.matmul(
                                ps[:, 3 * parity + c, 0:CH], w, x[:, k, CH * c:CH * c + CH],
                                start=(k == 0 and w is wh and x is src_hi), stop=(k == kn - 1 and w is wl))
                return last

            def ab(n):
                return ((0, piece_split[0], n + 1), (4, piece_split[1], n + 1))

            def spread_rms(group):
                pe.wait_ge(rms_done, group + 1)
                for i in range(*RMS_GROUPS[group]):
                    c0, w = (P * (i - 1), P) if i else (SEQ, NS)
                    last = nc.tensor.matmul(flat(1)[:, c0:c0 + w], rms_rows[0:w, i, :], ident[0:w, 0:w],
                                            start=True, stop=True)
                last.then_inc(tile_done if group else rms_spread, 1)

            pe.wait_ge(con_loaded, 16)
            for t in (PBLK, *range(PBLK)):
                w = P if t < PBLK else NS
                pe.wait_ge(x_loaded[t], 16)
                if 2 <= t < PBLK:
                    pe.wait_ge(xb_copied, t - 1)
                col = 512 * X_BANK[t]
                for k in range(KT):
                    last = nc.tensor.transpose(psf[:, col + w * k:col + w * k + w], xr[0:w, t, P * k:P * k + P],
                                               ident[0:w, 0:w])
                last.then_inc(xb_done if t < PBLK else tile_done, 1)
                if t == PBLK // 2:
                    spread_rms(0)
            spread_rms(1)

            def turn(kind, j, i, r):
                ge(pe, round_free, r - 1)
                bank = 6 + r % 2
                if r < 2:
                    pe.wait_ge(hist_copied, 1)
                if kind == "rows":
                    src = sa[:, 7 * (j % 2), :]
                    if i == 0:
                        ge(pe, set_free[j % 2], (QKV_TILE + j) // 2 + 1)
                    for b in range(4 if i < 2 else 0):
                        last = nc.tensor.transpose(ps[:, bank, P * b:P * b + P],
                                                   src[:, P * (4 * i + b):P * (4 * i + b) + P], ident)
                    if i == 2:
                        last = nc.tensor.transpose(ps[0:NS, bank, 0:P], src[:, SEQ:T], ident)
                else:
                    if i == 0:
                        ge(pe, stack_done, j + 1)
                    src = st32[:, j % 2, :].rearrange("p (b h e) -> p b h e", h=2, e=P)
                    for b in range(4 if i < 4 else 0):
                        last = nc.tensor.transpose(ps[:, bank, P * b:P * b + P],
                                                   src[:, 4 * (i % 2) + b, i // 2, :], ident)
                    for b in range(2 if i == 4 else 0):
                        last = nc.tensor.transpose(ps[:, bank, NS * b:NS * b + NS], src[0:NS, PBLK, b, :],
                                                   ident[0:NS, 0:NS])
                last.then_inc(round_done, 1)

            pe.wait_ge(xb_copied, PBLK)
            for n in range(2):
                ge(pe, set_free[n], 1)
            for k in range(KT):
                if k % 4 == 0:
                    pe.wait_ge(piece_split[k // 4], 1)
                pe.wait_ge(m_ready, k + 1)
                for h in range(2):
                    last = products(h, 0, h, m_hi, m_lo, k)
                    if k == KT - 1:
                        last.then_inc(tile_done, 1)
            pe.wait_ge(hist_loaded, 16)
            for k in range(KT):
                last = nc.tensor.transpose(ps[:, 6 + k // 4, nh * (k % 4):nh * (k % 4) + nh],
                                           state_rows[0:nh, P * k:P * k + P], ident[0:nh, 0:nh])
            last.then_inc(hist_done, 1)

            def rounds(plan):
                after = {}
                for step, kind, jj, i, r in plan:
                    if kind == "std":
                        continue
                    after.setdefault(step, []).append(lambda a=(kind, jj, i, r): turn(*a))
                return after

            for j in range(2, 12):
                project(j % 2, (QKV_TILE + j) // 2, (j // 2) % 2, j % 2, m_hi, m_lo,
                        pieces=ab(j // 2), after=rounds(PLAN[j]), done=True)

            def turn_keys(i, g):
                pe.wait_ge(round_free, ROUNDS)
                pe.wait_ge(kc_loaded[g], i * 16 + 16)
                for p in range(NB // 2):
                    last = nc.tensor.transpose(ps[:, 6, P * p:P * p + P],
                                               kc[:, g, 2 * p:2 * p + 2, :].rearrange("p b e -> p (b e)"), ident)
                last.then_inc(samp_done, 1)

            def sample_scores(v, r):
                if r == 0:
                    pe.wait_ge(samp_out, v + 1)
                    pe.wait_ge(key_copied, v + 1)
                if r == 2:
                    pe.wait_ge(s_read, v * 3 + 1)
                q = q_group[:, r % 2, :]
                keys = kts[:] if r < 2 else k_new[:, NS * v:NS * v + NS]
                nc.tensor.matmul(ps[:, (7, 6, 7)[r], 0:(512, 512, NS)[r]], q, keys, start=True, stop=True)\
                    .then_inc(samp_done, 1)

            def turn_sample_probs(v, r):
                if r == 0:
                    pe.wait_ge(s_prob, v + 1)
                if r == 2:
                    pe.wait_ge(spt_copied, v * 3 + 1)
                for b in range(4 * r, min(4 * r + 4, NB + 1)):
                    w = P if b < NB else NS
                    last = nc.tensor.transpose(ps[0:w, (6, 7, 6)[r], P * (b % 4):P * (b % 4) + P],
                                               sprob[:, P * b:P * b + w], ident)
                last.then_inc(samp_done, 1)

            def sample_values(v, i, g):
                pe.wait_ge(spt_copied, v * 3 + 3)
                pe.wait_ge(vc_loaded[g], i * 32 + 32)
                for b, seq in enumerate(SEQ_ORDER):
                    nc.tensor.matmul(ps[:, 7, 0:P], vc[:, g, seq].rearrange("p c e -> p (c e)"), spt[:, b, :],
                                     start=(b == 0), stop=False)
                for part in range(2):
                    new = v_group[0:NS, part].rearrange("p c e -> p (c e)")
                    last = nc.tensor.matmul(ps[:, 7, 0:P], new, spt[0:NS, NB, :], start=False, stop=(part == 1))
                last.then_inc(samp_done, 1)

            for i in range(2):
                for h in range(4):
                    g = h // 2
                    v = i * 2 + g
                    if h % 2 == 0:
                        after = {3: [lambda i=i, g=g: turn_keys(i, g)],
                                 6: [lambda v=v: sample_scores(v, 0), lambda v=v: sample_scores(v, 1)],
                                 7: [lambda v=v: sample_scores(v, 2)]}
                        if v == 0:
                            for step, calls in rounds(PLAN[12]).items():
                                after[step] = calls + after.get(step, [])
                    else:
                        after = {4: [lambda v=v: turn_sample_probs(v, 0), lambda v=v: turn_sample_probs(v, 1)],
                                 5: [lambda v=v: turn_sample_probs(v, 2)],
                                 7: [lambda v=v, i=i, g=g: sample_values(v, i, g)]}
                    project(h % 2, i * 2 + (GATE_TILE // 2 + h // 2), h // 2, h % 2, m_hi, m_lo,
                            pieces=ab(i * 2 + (GATE_CHUNK + h // 2)), after=after, done=True)

            def round_of(kind, u, s, m, first=False):
                r = att_round(kind, u) + s
                if not isinstance(r, int) or r >= 2:
                    pe.wait_ge(att_read, r if kind == "V" else r - 1)
                return 6 + (att_bank(kind, m, first) + s) % 2

            def scores(u, m, t, s, first=False):
                slot, kv = m % 2, m % 4
                if first:
                    pe.wait_ge(samp_out, NKV + 1)
                    pe.wait_ge(zero_done, 1)
                if s == 0:
                    pe.wait_ge(unit_loaded[kv], t * 48 + 48)
                bank = round_of("S", u, s, m, first)
                for g in (2 * s, 2 * s + 1):
                    for part in range(2):
                        last = nc.tensor.matmul(ps[:, bank, 256 * (g % 2):256 * (g % 2) + 256], qt[:, slot, g, :],
                                                kt[:, kv, part, :, :].rearrange("p s n -> p (s n)"),
                                                start=(part == 0), stop=(part == 1))
                last.then_inc(att_done, 1)

            def turn_probs(u, m, s):
                if s == 0:
                    pe.wait_ge(prob_done, u + 1)
                bank = round_of("T", u, s, m)
                for g in range(G):
                    last = nc.tensor.transpose(ps[:, bank, P * g:P * g + P], prob[:, m % 2, g, P * s:P * s + P], ident)
                last.then_inc(att_done, 1)

            def values(u, m, t):
                kv = m % 4
                bank = round_of("V", u, 0, m)
                pe.wait_ge(v_loaded[kv], t * 32 + 32)
                if isinstance(u, int) and u == 0:
                    pe.wait_ge(zero_done, 2)
                for s in range(2):
                    for a, b in ((0, pt_hi), (0, pt_lo), (1, pt_hi)):
                        last = nc.tensor.matmul(ps[:, bank, :], vt[:, s, kv, P * a:P * a + P], b[s][:],
                                                start=(s == 0 and a == 0 and b is pt_hi),
                                                stop=(s == 1 and a == 1))
                last.then_inc(att_done, 1)

            def attention_half(i, m, k0, first):
                u, t = i * 8 + m, i * 2 + m // 4
                after = {k0: [], k0 + 1: [], k0 + 2: []}
                if not first or m >= 2:
                    after[k0].append(lambda: values(u - 2, (m - 2) % 8, t if m % 4 >= 2 else t - 1))
                after[k0 + (1 if first and m == 0 else 0)].append(lambda: scores(u, m, t, 0, first and m == 0))
                after[k0 + 1].append(lambda: scores(u, m, t, 1, first and m == 0))
                if not first or m >= 1:
                    for s in range(2):
                        after[k0 + 2].append(lambda s=s: turn_probs(u - 1, (m - 1) % 8, s))
                return after

            def attention_tiles(i, first=False):
                for h in range(4):
                    after = attention_half(i, 2 * h, 0, first) | attention_half(i, 2 * h + 1, 4, first)
                    project(h % 2, i * 2 + ((GATE_TILE + KT) // 2 + h // 2), h // 2, h % 2, m_hi, m_lo,
                            pieces=ab(i * 2 + (GATE_CHUNK + 4 + h // 2)), after=after, done=True)

            attention_tiles(0, first=True)
            with pe.Fori(1, PBLK // 2) as i:
                attention_tiles(i)

            def turn_history(h, value):
                ge(pe, keep_ready, value)
                pe.wait_ge(pool_copied, value)
                nc.tensor.transpose(ps[0:nh, 6, 0:P], keep[:, h, :], ident)
                nc.tensor.transpose(ps[0:HIST, 6, P:2 * P], ub[:, h, SEQ:SEQ + HIST], ident).then_inc(pool_t, 1)

            def pool_group(g, tail=None):
                half = g * 3 + POOL_TILE // 2
                for h in range(2):
                    project(h, half, 0, h, m_hi, m_lo, pieces=ab(g * 2 + POOL_CHUNK), after=tail if h == 0 else None,
                            done=True)
                for h in range(2):
                    project(h, half + 1, 1, h, m_hi, m_lo, pieces=ab(g * 2 + (POOL_CHUNK + 1)), used=(h == 1),
                            after={3: [lambda h=h: turn_history(h, g * 2 + (h + 1))]}, done=True)
                for h in range(2):
                    pe.wait_ge(r_ready, g * 2 + 2)
                    project(h, half + 2, 1, h, r_hi, r_lo, k0=KT, kn=XKT,
                            pieces=((0, piece_split[2], g + 1),), done=True)

            end = PBLK * NKV
            pool_group(0, {0: [lambda: values(end - 2, 6, PBLK - 1)],
                           2: [lambda: turn_probs(end - 1, 7, 0), lambda: turn_probs(end - 1, 7, 1)],
                           5: [lambda: values(end - 1, 7, PBLK - 1)]})
            with pe.Fori(1, 4) as g:
                pool_group(g)

            def stage(base, chunk, fills):
                with pe.Fori(0, 2) as i:
                    for h in range(4):
                        project(h % 2, i * 2 + (base // 2 + h // 2), h // 2, h % 2, m_hi, m_lo,
                                wait_m=KT * fills if h == 0 else None, used=(h == 3),
                                pieces=ab(i * 2 + (chunk + h // 2))).then_inc(tile_done, 1)

            stage(PP_TILE, PP_CHUNK, 1)
            stage(PA_TILE, PA_CHUNK, 2)
            def turn_p(r):
                k, i = divmod(r, 3)
                pe.wait_ge(p_loaded, 16 * (PBLK + 1))
                ge(pe, p_round_free, r - 1)
                for b in range(4 if i < 2 else 0):
                    last = nc.tensor.transpose(ps[:, 6 + r % 2, P * b:P * b + P],
                                               yrow[:, 4 * i + b, P * k:P * k + P], ident)
                if i == 2:
                    last = nc.tensor.transpose(ps[:, 6 + r % 2, 0:NS], yrow[0:NS, PBLK, P * k:P * k + P],
                                               ident[0:NS, 0:NS])
                last.then_inc(p_round, 1)

            for j in range(KT):
                project(j % 2, WO_TILE // 2 + j // 2, j // 2 % 2, j % 2, m_hi, m_lo, wait_m=KT * 3 if j == 0 else None,
                        used=(j == KT - 1), pieces=ab(WO_CHUNK + j // 2), done=True,
                        after={1 + r: [lambda r=r: turn_p(r)] for r in range(6)} if j == KT - 2 else None)

            def turn_y(h, r, need, i):
                if i == 0:
                    ge(pe, yt_done, need)
                ge(pe, y_round_free, r - 1)
                bank = 6 + (3 * h + i) % 2
                for b in range(4 if i < 2 else 0):
                    t = 4 * i + b
                    last = nc.tensor.transpose(ps[:, bank, P * b:P * b + P], yt[:, h, P * t:P * t + P], ident)
                if i == 2:
                    last = nc.tensor.transpose(ps[0:NS, bank, 0:P], yt[:, h, SEQ:T], ident)
                last.then_inc(y_round, 1)

            def final_chunk(c, slot, first=False):
                for h in range(2):
                    j = c * 2 + h
                    after = {}
                    if not first or h:
                        hh = 1 - h
                        after = {4 + i: [lambda i=i, j=j, hh=hh: turn_y(hh, (j - 1) * 3 + i, j, i)] for i in range(3)}
                    half = c * 2 + (FIN_TILE // 2 + h)
                    project(0, half, slot, h, m_hi, m_lo, wait_m=4 * KT if h == 0 else None,
                            pieces=ab(c + FIN_CHUNK), after=after).then_inc(tile_done, 1)
                    pe.wait_ge(p_round_free, 6)
                    project(1, half, slot, h, p_hi, p_lo, k0=KT, kn=XKT,
                            pieces=((0, piece_split[2], c + 5),)).then_inc(tile_done, 1)

            final_chunk(0, 0, first=True)
            final_chunk(1, 1)
            with pe.Fori(1, 2) as i:
                for h in range(2):
                    final_chunk(i * 2 + h, h)
            for i in range(3):
                turn_y(1, 21 + i, 8, i)

        @block.vector
        def _(dve):
            v = nc.vector
            step = Steps(dve, dve_step)

            def split_lo(k, value):
                dve.wait_ge(m_hi_done, value)
                v.tensor_tensor(m_lo[:, k, :], sa[:, k, :], m_hi32[:, k, :], ALU.subtract).then_inc(m_ready, 1)

            step.did(v.memset(rs[:, 0, :], 1.0))
            step.did(v.memset(warm[:], 0.0))
            step.settle()
            v.memset(rs[:, 1, :], 1.0).then_inc(ssq_init, 1)
            dve.wait_ge(tile_done, 1)
            v.tensor_copy(sa[:, :, SEQ:T], psf[:, 0:KT * NS].rearrange("p (k n) -> p k n", n=NS))\
                .then_inc(set_free[0], 1)
            for t in range(PBLK):
                dve.wait_ge(xb_done, t + 1)
                col = 512 * X_BANK[t]
                v.tensor_copy(sa[:, :, P * t:P * t + P], psf[:, col:col + D].rearrange("p (k n) -> p k n", n=P))\
                    .then_inc(xb_copied, 1)
                if t in (PBLK // 2 - 1, PBLK - 1):
                    group = t // (PBLK // 2)
                    a, b = RMS_GROUPS[group]
                    dve.wait_ge(ssq_done, b + 1)
                    v.tensor_scalar(rs[:, 1, a:b], rs[:, 0, a:b], 1.0 / D, EPS, ALU.mult, ALU.add).then_inc(ms_done, 1)
                    dve.wait_ge(std_done, group + 1)
                    step.did(v.reciprocal(rs[:, 3, a:b], rs[:, 2, a:b]))
                    step.settle()
                    v.tensor_copy(rms_rows[:, a:b], rs[:, 3, a:b].unsqueeze(2).to_broadcast([P, b - a, P]))\
                        .then_inc(rms_done, 1)
            dve.wait_ge(rms_spread, 1)
            v.tensor_copy(rbc[:, 0:512], flat(1)[:, 0:512])
            step.did(v.tensor_copy(rbc[:, SEQ:T], flat(1)[:, SEQ:T]))
            dve.wait_ge(tile_done, 2)
            v.tensor_copy(rbc[:, 512:SEQ], flat(1)[:, 512:SEQ]).then_inc(set_free[1], 1)
            step.settle()
            dve.wait_ge(set_free[1], 1)
            dve.wait_ge(set_free[0], 1)
            dve.wait_ge(xb_copied, PBLK)
            dve.wait_ge(par_loaded, 16)
            for k in range(KT + 1):
                if k < KT:
                    if k >= 2:
                        dve.wait_ge(m_ready, k - 1)
                    v.scalar_tensor_tensor(xn[:, k % 2, :], sa[:, k, :], g8[:, k:k + 1], rbc[:], ALU.mult, ALU.mult)\
                        .then_inc(xn_done, 1)
                if k:
                    dve.wait_ge(m_hi_done, k)
                    v.tensor_tensor(m_lo[:, k - 1, :], xn[:, (k - 1) % 2, :], m_hi32[:, k - 1, :], ALU.subtract)\
                        .then_inc(m_ready, 1)

            step.did(v.tensor_scalar(qg, qg, HD ** -0.5, None, ALU.mult))
            dve.wait_ge(m_ready, KT)
            dve.wait_ge(xt_stored, 16 * (KT // 2))
            v.memset(rows[:, :, PBLK * P:], 1.0).then_inc(rows_init, 1)
            step.settle()
            sq = saf[:, 1056:1056 + 1152].rearrange("p (a e) -> p a e", e=HD)
            tmp = [saf[:, 2304 + 144 * i:2304 + 144 * i + 144].rearrange("p (a e) -> p a e", e=8) for i in range(4)]

            def heads(par):
                return rows[:, par, :].rearrange("p (a e) -> p a e", e=HD)

            def keep_kv(j):
                col = P * (j - 8)
                v.tensor_copy(kv_out[:, 0, col:col + P], rows[:, j % 2, 7 * P:8 * P])
                v.tensor_copy(kv_out[0:NS, 1, col:col + P], rows[0:NS, j % 2, 8 * P:9 * P]).then_inc(kv_kept, 1)

            def split_rows(j):
                hi, lo = (stack[:, j % 2, :].rearrange("p (a s e) -> p a s e", s=2, e=HD)[:, :, s] for s in (0, 1))
                hi32 = st32[:, j % 2, :].rearrange("p (a s e) -> p a s e", s=2, e=HD)[:, :, 0]
                x = heads(j % 2)
                if j >= 2:
                    dve.wait_ge(round_done, BACK_END[j - 2])
                step.did(v.tensor_copy(hi, x))
                step.settle()
                v.tensor_tensor(lo, x, hi32, ALU.subtract).then_inc(stack_done, 1)

            for j in range(12):
                x = heads(j % 2)
                dve.wait_ge(round_free, ROWS_END[j])
                if j < 10:
                    step.did(v.tensor_tensor(sq, x, x, ALU.mult))
                    step.settle()
                    step.did(v.tensor_reduce(hs[:, 0, :], sq, AX_X, ALU.add))
                    step.settle()
                    v.tensor_scalar(hs[:, 1, :], hs[:, 0, :], 1.0 / HD, EPS, ALU.mult, ALU.add).then_inc(hms_done, 1)
                    gain = (qg if j < 8 else kg).unsqueeze(1).to_broadcast([P, 18, HD])
                    step.did(v.tensor_tensor(x, x, gain, ALU.mult))
                    dve.wait_ge(hstd_done, j + 1)
                    step.did(v.reciprocal(hs[:, 3, :], hs[:, 2, :]))
                    step.settle()
                    step.did(v.tensor_tensor(x, x, hs[:, 3, :].unsqueeze(2).to_broadcast([P, 18, HD]), ALU.mult))
                    step.settle()
                    x1, x2 = x[:, :, 0:8], x[:, :, 8:16]
                    for o, a, b in zip(tmp, (x1, x2, x2, x1), (cosv, sinv, cosv, sinv)):
                        last = v.tensor_tensor(o, a, b, ALU.mult)
                    step.did(last)
                    step.settle()
                    v.tensor_tensor(x1, tmp[0], tmp[1], ALU.subtract)
                    step.did(v.tensor_tensor(x2, tmp[2], tmp[3], ALU.add))
                    step.settle()
                if j >= 8:
                    keep_kv(j)
                split_rows(j)

            dve.wait_ge(q_loaded, 16 * 8)
            v.memset(q_group[HD:P, 0, :], 0.0)
            v.memset(q_group[0:HD, 1, :], 0.0)
            v.tensor_tensor(q_sum[:], q_sum[:], q_low[:], ALU.add).then_inc(samp_out, 1)
            dve.wait_ge(smask_loaded, 16)
            with dve.Fori(0, NKV) as kv:
                step.loop(kv, 0, 6)
                ge(dve, samp_done, kv * 8 + 2)
                for r, (bank, c0, w) in enumerate(((7, 0, 512), (6, 512, 512), (7, SEQ, NS))):
                    if r:
                        dve.wait_ge(samp_done, kv * 8 + (2 + r))
                    v.tensor_tensor(sprob[:, c0:c0 + w], ps[:, bank, 0:w], smsk[:, c0:c0 + w], ALU.add)\
                        .then_inc(s_read, 1)
                dve.wait_ge(s_read, kv * 3 + 3)
                step.did(v.tensor_reduce(sst[:, 0:1], sprob[:], AX_X, ALU.max))
                step.did(v.tensor_copy(sst[:, 7:8], sinks_s[:, bass.ds(kv, 1)]))
                step.settle()
                step.did(v.tensor_tensor(sst[:, 6:7], sst[:, 0:1], sst[:, 7:8], ALU.max))
                step.settle()
                v.tensor_scalar(sst[:, 1:2], sst[:, 6:7], -1.0, None, ALU.mult)
                v.tensor_tensor(sst[:, 2:3], sst[:, 7:8], sst[:, 6:7], ALU.subtract).then_inc(s_shift, 1)
                dve.wait_ge(s_exp, kv + 1)
                step.did(v.tensor_tensor(sst[:, 5:6], sst[:, 3:4], sst[:, 4:5], ALU.add))
                step.settle()
                step.did(v.reciprocal(sst[:, 6:7], sst[:, 5:6]))
                step.settle()
                v.tensor_scalar(sprob[:], sprob[:], sst[:, 6:7], None, ALU.mult).then_inc(s_prob, 1)
                dve.wait_ge(samp_done, kv * 8 + 8)
                for q in range(2):
                    half = slice(64 * q, 64 * q + 64)
                    o = ps[half, 7, 0:P].rearrange("p (a q n) -> p q a n", q=2, n=NS)[:, q]
                    last = v.tensor_copy(s_out[half, bass.ds(kv * 2, 2), :], o)
                last.then_inc(samp_out, 1)
                step.did(v.memset(sst[:, 0:1], 0.0))
            step.leave(NKV, 6)
            v.memset(kt[:, :, :, 1, :].bitcast(F32), 0.0).then_inc(zero_done, 1)
            tile_free(dve, GATE_TILE + 6)
            tile_free(dve, GATE_TILE + 7)
            dve.wait_ge(samp_out, NKV + 1)
            step.did(v.tensor_tensor(sa[:, :, SEQ:T], sa[:, :, SEQ:T], s_out[:], ALU.mult))
            step.settle()
            v.memset(vt[:, 1, :, :].bitcast(F32), 0.0).then_inc(zero_done, 1)

            dve.wait_ge(masks_loaded, 16)
            dve.wait_ge(zero_done, 2)

            def mask_scores(u, m, mask, first):
                slot, kv = m % 2, m % 4
                for s in range(2):
                    n = att_round("S", u) + s + 1
                    dve.wait_ge(att_done, n)
                    v.tensor_copy(st[:, slot, 5, 2 * s:2 * s + 2], sinks[:, G * kv + 2 * s:G * kv + 2 * s + 2])
                    for g in (2 * s, 2 * s + 1):
                        bank = 6 + (att_bank("S", m, first) + s) % 2
                        last = v.tensor_tensor_reduce(
                            prob[:, slot, g, :], ps[:, bank, 256 * (g % 2):256 * (g % 2) + 256],
                            msk[:, mask, :], 1.0, sinks[:, G * kv + g:G * kv + g + 1], ALU.add, ALU.max,
                            st[:, slot, 0, g:g + 1])
                    last.then_inc(att_read, 1)
                dve.wait_ge(att_read, n)
                v.tensor_scalar(st[:, slot, 1, :], st[:, slot, 0, :], -1.0, None, ALU.mult)
                v.tensor_tensor(st[:, slot, 2, :], sinks[:, G * kv:G * kv + G], st[:, slot, 0, :], ALU.subtract)\
                    .then_inc(shift_done, 1)

            def split_probs(u, m):
                for s in range(2):
                    ge(dve, pt_hi_done, u * 2 + (s + 1))
                    bank = 6 + (att_bank("T", m) + s) % 2
                    v.tensor_tensor(pt_lo[s][:], ps[:, bank, :], pt_hi[s][:].bitcast(F32), ALU.subtract)\
                        .then_inc(att_read, 1)

            def gate_output(u, m, tok):
                kv = m % 4
                dve.wait_ge(att_done, att_round("V", u) + 1)
                for q in range(2):
                    half = slice(64 * q, 64 * q + 64)
                    o = ps[half, att_bank("V", m), :].rearrange("p (a q n) -> p q a n", q=2, n=P)[:, q]
                    dst = sa[half, 2 * kv:2 * kv + 2, tok]
                    last = v.tensor_tensor(dst, o, dst, ALU.mult)
                last.then_inc(att_read, 1)

            def normalise(u, m):
                slot = m % 2
                dve.wait_ge(exp_done, u + 1)
                step.did(v.tensor_tensor(st[:, slot, 0, :], st[:, slot, 3, :], st[:, slot, 4, :], ALU.add))
                step.settle()
                step.did(v.reciprocal(st[:, slot, 5, :], st[:, slot, 0, :]))
                step.settle()
                for g in range(G):
                    last = v.tensor_scalar(prob[:, slot, g, :], prob[:, slot, g, :], st[:, slot, 5, g:g + 1],
                                           None, ALU.mult)
                last.then_inc(prob_done, 1)

            def attention_half(i, m, first=False):
                u = i * 8 + m
                if not first or m >= 2:
                    tok = bass.ds(i * (2 * P) + ((m - 2) // 4) * P, P)
                    gate_output(u - 2, (m - 2) % 8, tok)
                mask_scores(u, m, 1 if m >= 4 else (0 if first else 2), first and m == 0)
                if not first or m >= 1:
                    split_probs(u - 1, (m - 1) % 8)
                normalise(u, m)

            for m in range(8):
                attention_half(0, m, first=True)
            with dve.Fori(1, PBLK // 2) as i:
                step.loop(i, 1, 16)
                for m in range(8):
                    attention_half(i, m)
            step.leave(PBLK // 2 - 1, 16)
            end, last_tok = PBLK * NKV, slice(SEQ - P, SEQ)
            gate_output(end - 2, 6, last_tok)
            split_probs(end - 1, 7)
            gate_output(end - 1, 7, last_tok)
            dve.wait_ge(att_read, ATT_ROUNDS)

            for g in range(4):
                w = 2 << g
                for h in range(2):
                    tile_free(dve, POOL_TILE + 6 * g + h)
                    ge(dve, r_ready, 2 * g + h)
                    src, dst, d = ub[:, h, :], wa[:], 1
                    while d < w:
                        step.did(v.tensor_tensor(dst[:, 2 * d - 1:], src[:, 2 * d - 1:], src[:, d - 1:UL - d], ALU.add))
                        step.settle()
                        src, dst, d = dst, (wb[:] if d in (1, 4) else wa[:]), 2 * d
                    r = dst[:, 0:T]
                    v.scalar_tensor_tensor(r[:, 0:SEQ], src[:, HIST:HIST + SEQ], 1.0 / w, ub[:, h, HIST:HIST + SEQ],
                                           ALU.mult, ALU.subtract)
                    step.did(v.scalar_tensor_tensor(
                        r[:, SEQ:T].rearrange("p (b n) -> p b n", n=NT),
                        src[:, HIST + SEQ:UL].rearrange("p (b n) -> p b n", n=SEG)[:, :, HIST:SEG], 1.0 / w,
                        ub[:, h, HIST + SEQ:UL].rearrange("p (b n) -> p b n", n=SEG)[:, :, HIST:SEG],
                        ALU.mult, ALU.subtract))
                    step.settle()
                    step.did(v.tensor_tensor(r[:, 0:w - 1], src[:, HIST:HIST + w - 1], rcv[:, 0:w - 1], ALU.mult))
                    step.settle()
                    step.did(v.tensor_tensor(r[:, 0:w - 1], r[:, 0:w - 1], ub[:, h, HIST:HIST + w - 1], ALU.subtract))
                    step.settle()
                    ge(dve, tile_done, POOL_TILE + 6 * g)
                    step.did(v.tensor_copy(r_hi[:, h, :], r))
                    step.settle()
                    v.tensor_tensor(r_lo[:, h, :], r, r_hi32[:, h, :], ALU.subtract).then_inc(r_ready, 1)
                if g == 3:
                    for kk in range(6):
                        split_lo(kk, KT + kk + 1)
                for h in range(2):
                    n = POOL_TILE + 6 * g + 4 + h
                    k = 2 * g + h
                    dve.wait_ge(tile_done, n + 1)
                    tile_free(dve, n - 2)
                    if g == 0 and h == 0:
                        dve.wait_ge(yb_stored, 16)
                    v.scalar_tensor_tensor(thirds(sa[:, k, :]), pset(n), ps8[:, k:k + 1], thirds(zs[:, h, :]),
                                           ALU.mult, ALU.mult).then_inc(set_free[h], 1)
                    if g == 3:
                        split_lo(k, KT + k + 1)

            dve.wait_ge(pool_stored, 16 * 2 * KT)

            def gated(base, m, j, par, half, second):
                dve.wait_ge(tile_done, j + (base + 1))
                dve.wait_ge(gin_loaded[par], m)
                out = mix[:, j, :] if isinstance(j, int) else mix[:, bass.ds(j, 1), :].rearrange("p a n -> p (a n)")
                if not second:
                    v.tensor_tensor(thirds(out), pset(par), thirds(gin[:, par, :]), ALU.mult)\
                        .then_inc(set_free[par], 1)
                else:
                    if not (isinstance(j, int) and j == 0):
                        step.settle()
                    v.tensor_tensor(thirds(gtmp[:]), pset(par), thirds(gin[:, par, :]), ALU.mult)\
                        .then_inc(set_free[par], 1)
                    dve.wait_ge(set_free[par], half + (base // 2 + 1))
                    step.did(v.tensor_tensor(out, out, gtmp[:], ALU.add))

            def stage(base, loads, second):
                with dve.Fori(0, 3) as i:
                    if second:
                        step.loop(i, 0, 2)
                    for h in range(2):
                        gated(base, (i + loads) * 16 + 16, i * 2 + h, h, i, second)
                if second:
                    step.leave(3, 2)

            stage(PP_TILE, 0, False)
            gated(PP_TILE, 64, 6, 0, 3, False)
            for k in range(7):
                split_lo(k, 2 * KT + k + 1)
            gated(PP_TILE, 64, 7, 1, 3, False)
            split_lo(7, 3 * KT)

            stage(PA_TILE, 4, True)
            gated(PA_TILE, 128, 6, 0, 3, True)
            step.settle()

            def split_mix(k):
                dve.wait_ge(m_hi_done, 3 * KT + k + 1)
                v.tensor_tensor(m_lo[:, k, :], mix[:, k, :], m_hi32[:, k, :], ALU.subtract).then_inc(m_ready, 1)

            v.memset(gtmp[:, 0:1], 0.0).then_inc(mix_ready, 1)
            for k in range(7):
                split_mix(k)
            gated(PA_TILE, 128, 7, 1, 3, True)
            step.settle()
            v.memset(gtmp[:, 0:1], 0.0).then_inc(mix_ready, 1)
            split_mix(7)

            def residual(m, j, par):
                dve.wait_ge(tile_done, j + (WO_TILE + 1))
                dve.wait_ge(gin_loaded[par], m)
                out = sa[:, j, :] if isinstance(j, int) else sa[:, bass.ds(j, 1), :].rearrange("p a n -> p (a n)")
                v.tensor_tensor(thirds(out), pset(par), thirds(gin[:, par, :]), ALU.add).then_inc(set_free[par], 1)

            with dve.Fori(0, 3) as i:
                for h in range(2):
                    residual((i + 8) * 16 + 16, i * 2 + h, h)
            for r in range(6):
                k, i = divmod(r, 3)
                dve.wait_ge(p_half, r + 1)
                c0, w = 512 * i, (512 if i < 2 else NS)
                v.tensor_tensor(p_lo[:, k, c0:c0 + w], ps[:, 6 + r % 2, 0:w], p_hi32[:, k, c0:c0 + w],
                                ALU.subtract).then_inc(p_round_free, 1)
            residual(192, 6, 0)
            for k in range(7):
                split_lo(k, 4 * KT + k + 1)
            residual(192, 7, 1)
            split_lo(7, 5 * KT)

            def final(j, par):
                n = j * 2 + (FIN_TILE + 1)
                ge(dve, y_round, (j - 1) * 3)
                dyn = not isinstance(j, int)
                hi = m_hi32[:, bass.ds(j, 1), :].rearrange("p a n -> p (a n)") if dyn else m_hi32[:, j, :]
                lo = m_lo32[:, bass.ds(j, 1), :].rearrange("p a n -> p (a n)") if dyn else m_lo32[:, j, :]
                step.did(v.tensor_tensor(yt[:, par, :], hi, lo, ALU.add))
                dve.wait_ge(tile_done, n + 1)
                dve.wait_ge(set_free[0], j + (FIN_TILE // 2 + 1))
                v.tensor_tensor(thirds(gin[:, par, :]), pset(1), thirds(sg[:]), ALU.mult).then_inc(set_free[1], 1)
                step.settle()
                dve.wait_ge(set_free[1], j + (FIN_TILE // 2 + 1))
                v.tensor_tensor(yt[:, par, :], yt[:, par, :], gin[:, par, :], ALU.add).then_inc(yt_done, 1)

            final(0, 0)
            final(1, 1)
            with dve.Fori(1, 4) as i:
                step.loop(i, 1, 2)
                for h in range(2):
                    final(i * 2 + h, h)
            step.leave(3, 2)

        @block.scalar
        def _(act):
            a = nc.scalar

            def split_hi(k, src, used=None, end=None):
                if used is not None:
                    ge(act, *((m_used, used + k + 1) if k < KT - 1 else (tile_done, end)))
                a.activation(m_hi[:, k, :], src[:, k, :], ACT.Copy).then_inc(m_hi_done, 1)

            act.wait_ge(ssq_init, 1)
            a.activation(rs[:, 2, :], rs[:, 1, :], ACT.Sqrt).then_inc(ssq_done, 1)
            for i, t in enumerate((PBLK, *range(PBLK))):
                w = P if t < PBLK else NS
                act.wait_ge(x_loaded[t], 16)
                act.wait_ge(ssq_done, i + 1)
                a.activation(state_rows[0:w, :], xr[0:w, t, :], ACT.Square, accum_out=rs[0:w, 0, i:i + 1])\
                    .then_inc(ssq_done, 1)
                if i + 1 in (RMS_GROUPS[0][1], RMS_GROUPS[1][1]):
                    group = i // RMS_GROUPS[0][1]
                    c0, c1 = RMS_GROUPS[group]
                    act.wait_ge(ms_done, group + 1)
                    a.activation(rs[:, 2, c0:c1], rs[:, 1, c0:c1], ACT.Sqrt).then_inc(std_done, 1)
            for k in range(KT):
                act.wait_ge(xn_done, k + 1)
                a.activation(m_hi[:, k, :], xn[:, k % 2, :], ACT.Copy).then_inc(m_hi_done, 1)

            act.wait_ge(rows_init, 1)
            act.wait_ge(xt_stored, 16 * (KT // 2))

            def take(kind, j, i, r):
                act.wait_ge(round_done, r + 1)
                bank = 6 + r % 2
                if kind == "rows":
                    if i == 0:
                        ge(act, stack_done, j - 1)
                    if i < 2:
                        ins = a.activation(rows[:, j % 2, 512 * i:512 * i + 512], ps[:, bank, :], ACT.Copy)
                    else:
                        ins = a.activation(rows[0:NS, j % 2, SEQ:SEQ + P], ps[0:NS, bank, 0:P], ACT.Copy)
                    ins.then_inc(round_free, 1)
                    return
                if i == 0:
                    ge(act, qk_stored, 16 * j)
                if i < 4:
                    dst = qkst[:, i // 2, 512 * (i % 2):512 * (i % 2) + 512]
                    src = ps[:, bank, :]
                else:
                    dst = qkst[:, :, SEQ:T]
                    src = ps[:, bank, 0:NS * 2].rearrange("p (s n) -> p s n", n=NS)
                a.activation(dst, src, ACT.Copy).then_inc(round_free, 1)
                if i == 4:
                    act.wait_ge(round_free, r + 1)
                    act.dma_start(qk_d[2 * j:2 * j + 2].rearrange("h p n -> p h n"), qkst[:].bitcast(F32))\
                        .then_inc(qk_stored, 16)

            def head_std(j):
                act.wait_ge(hms_done, j + 1)
                a.activation(hs[:, 2, :], hs[:, 1, :], ACT.Sqrt).then_inc(hstd_done, 1)

            def store_v(j):
                act.wait_ge(stack_done, j + 1)
                act.dma_start(v_d[:, :, 2 * (j - 10):2 * (j - 10) + 2, :].rearrange("b p v e -> p b (v e)"),
                              st32[:, j % 2, :].rearrange("p (b e) -> p b e", e=256)).then_inc(v_stored, 16)

            for j in range(13):
                for _, kind, jj, i, r in PLAN[j]:
                    if kind == "std":
                        head_std(jj)
                    else:
                        take(kind, jj, i, r)
                if j < 12:
                    act.wait_ge(tile_done, QKV_TILE + j + 1)
                    a.activation(thirds(sa[:, 7 * (j % 2), :]), pset(j), ACT.Copy).then_inc(set_free[j % 2], 1)
                if j == 1:
                    act.wait_ge(hist_done, 1)
                    a.activation(hist[:].rearrange("p (a k) n -> p a (k n)", a=2), ps[:, 6:8, 0:4 * nh], ACT.Copy)\
                        .then_inc(hist_copied, 1)
                if j == 11:
                    store_v(10)
            store_v(11)

            def silu(i, h):
                act.wait_ge(tile_done, i * 4 + (GATE_TILE + h + 1))
                out = sa[:, bass.ds(i * 4 + h, 1), :].rearrange("p a n -> p (a n)")
                a.activation(thirds(out), pset(h), ACT.Silu).then_inc(set_free[h % 2], 1)

            with act.Fori(0, 2) as i:
                for g in range(2):
                    kv = i * 2 + g
                    act.wait_ge(samp_out, kv + 1)
                    for part in range(2):
                        half = slice(HD * part, HD * part + HD)
                        a.activation(q_group[half, part, :], q_sum[half, bass.ds(kv * P, P)], ACT.Copy)
                    act.wait_ge(samp_done, kv * 8 + 1)
                    a.activation(kts[:], ps[:, 6, :], ACT.Copy).then_inc(key_copied, 1)
                    silu(i, 2 * g)
                    act.wait_ge(s_shift, kv + 1)
                    a.activation(sprob[:], sprob[:], ACT.Exp, bias=sst[:, 1:2], accum_out=sst[:, 3:4])
                    a.activation(sst[:, 4:5], sst[:, 2:3], ACT.Exp).then_inc(s_exp, 1)
                    act.wait_ge(v_new_loaded, 16)
                    new = v_new[0:NS, bass.ds(kv, 1), :].rearrange("p a (s e) -> p (a s) e", s=2)
                    for c in range(2):
                        a.activation(v_group[0:NS, :, c], new, ACT.Copy)
                    for r, (bank, rows_, w) in enumerate(((6, P, 4), (7, P, 4), (6, NS, 1))):
                        act.wait_ge(samp_done, kv * 8 + (5 + r))
                        a.activation(spt[0:rows_, 4 * r:4 * r + w, :],
                                     ps[0:rows_, bank, 0:P * w].rearrange("p (b n) -> p b n", n=P), ACT.Copy)\
                            .then_inc(spt_copied, 1)
                    silu(i, 2 * g + 1)

            act.wait_ge(zero_done, 2)

            def gate(m, h, half, before):
                act.wait_ge(tile_done, m + (GATE_TILE + KT + 1))
                if before is not None:
                    act.wait_ge(gate_stored[h], before * 16)
                a.activation(thirds(gst[:, h, :]), pset(h), ACT.Sigmoid).then_inc(set_free[h], 1)
                act.wait_ge(set_free[h], half + (GATE_TILE + KT) // 2 + 1)
                act.dma_start(gate_d[m], gst[:, h, :]).then_inc(gate_stored[h], 16)

            def hi_probs(u, m):
                for s in range(2):
                    act.wait_ge(att_done, att_round("T", u) + s + 1)
                    bank = 6 + (att_bank("T", m) + s) % 2
                    a.activation(pt_hi[s][:], ps[:, bank, :], ACT.Copy).then_inc(pt_hi_done, 1)

            warmed = Steps(act, warm_done)

            def exps(u, m):
                slot = m % 2
                act.wait_ge(shift_done, u + 1)
                for g in range(G):
                    a.activation(prob[:, slot, g, :], prob[:, slot, g, :], ACT.Exp, bias=st[:, slot, 1, g:g + 1],
                                 accum_out=st[:, slot, 3, g:g + 1])
                a.activation(st[:, slot, 4, :], st[:, slot, 2, :], ACT.Exp).then_inc(exp_done, 1)

            def attention_tiles(i, first=False):
                for m in range(8):
                    u = i * 8 + m
                    if not first or m >= 1:
                        hi_probs(u - 1, (m - 1) % 8)
                    exps(u, m)
                    if m % 2:
                        h = m // 2
                        gate(i * 4 + h, h % 2, i * 2 + h // 2, None if first and h < 2 else i * 2 + h // 2)
                        warmed.settle()
                        warmed.did(a.activation(warm[:, 1:2], warm[:, 0:1], ACT.Exp))

            attention_tiles(0, first=True)
            with act.Fori(1, PBLK // 2) as i:
                warmed.loop(i, 1, 4)
                attention_tiles(i)
            warmed.leave(PBLK // 2 - 1, 4)
            hi_probs(PBLK * NKV - 1, 7)

            act.wait_ge(att_read, ATT_ROUNDS)
            for h in range(2):
                act.wait_ge(gate_stored[h], 16 * KT)
            a.memzero(ub[:, :, 0:HIST]).then_inc(pool_copied, 1)
            act.wait_ge(pool_copied, 1)

            def take_history(k, need):
                act.wait_ge(pool_t, need)
                ge(act, pool_stored, 32 * (k))
                a.activation(pst[0:nh, 0, :], ps[0:nh, 6, 0:P], ACT.Copy)
                a.activation(pst[0:HIST, 1, :], ps[0:HIST, 6, P:2 * P], ACT.Copy).then_inc(pool_copied, 1)
                act.wait_ge(pool_copied, need + 1)
                cols = bass.ds(k * P, P)
                act.dma_start(npool_s[:, cols], pst[0:nh, 0, :]).then_inc(pool_stored, 16)
                act.dma_start(npool_p[:, cols], pst[0:HIST, 1, :]).then_inc(pool_stored, 16)

            def pool_group(g, first=False, last=False):
                for h in range(2):
                    k = g * 2 + h
                    act.wait_ge(tile_done, g * 6 + (POOL_TILE + h + 1))
                    if not first:
                        act.wait_ge(r_ready, g * 2 + (h - 1))
                    sam = ub[:, h, HIST + SEQ:UL].rearrange("p (b n) -> p b n", n=SEG)
                    old = hist[:, k, :] if first else hist[:, bass.ds(k, 1), :].rearrange("p a n -> p (a n)")
                    a.activation(sam[:, :, 0:HIST], old.rearrange("p (b n) -> p b n", n=HIST), ACT.Copy)
                    a.activation(ub[:, h, HIST:HIST + 2 * CH].rearrange("p (c n) -> p c n", n=CH),
                                 ps[:, 3 * h:3 * h + 2, 0:CH], ACT.Copy)
                    a.activation(ub[:, h, HIST + 2 * CH:HIST + SEQ], ps[:, 3 * h + 2, 0:SEQ - 2 * CH], ACT.Copy)
                    a.activation(sam[:, :, HIST:SEG],
                                 ps[:, 3 * h + 2, SEQ - 2 * CH:CH].rearrange("p (b n) -> p b n", n=NT), ACT.Copy)\
                        .then_inc(set_free[h], 1)
                    act.wait_ge(set_free[h], g * 3 + (POOL_TILE // 2 + 1))
                    a.activation(keep[:, h, :].rearrange("p (b n) -> p b n", n=HIST), sam[:, :, NT:SEG], ACT.Copy)\
                        .then_inc(keep_ready, 1)
                for h in range(2):
                    k = g * 2 + h
                    if last and h == 1:
                        for n in (16, 17):
                            tile_free(act, POOL_TILE + n)
                        for kk in range(6):
                            split_hi(kk, sa, 3 * (KT - 1), POOL_TILE + 22)
                    act.wait_ge(tile_done, g * 6 + (POOL_TILE + 2 + h + 1))
                    a.activation(thirds(zs[:, h, :]), pset(h), ACT.Silu).then_inc(set_free[h], 1)
                    take_history(k, k + 1)

            pool_group(0, first=True)
            with act.Fori(1, 3) as g:
                pool_group(g)
            pool_group(3, last=True)
            for k in range(6, KT):
                tile_free(act, POOL_TILE + 16 + k)
                split_hi(k, sa, 3 * (KT - 1), POOL_TILE + 22)
            act.wait_ge(yb_loaded, 16)
            for k in range(KT):
                split_hi(k, sa, 5 * (KT - 1), PA_TILE)
            for k in range(KT):
                ge(act, mix_ready, 1 if k < 7 else 2)
                split_hi(k, mix, 7 * (KT - 1), WO_TILE)
            for r in range(6):
                k, i = divmod(r, 3)
                c0, w = 512 * i, (512 if i < 2 else NS)
                act.wait_ge(p_round, r + 1)
                a.activation(p_hi[:, k, c0:c0 + w], ps[:, 6 + r % 2, 0:w], ACT.Copy).then_inc(p_half, 1)
            for k in range(KT):
                if k in (0, 7):
                    tile_free(act, WO_TILE + 6 + k // 7)
                split_hi(k, sa, 8 * (KT - 1), FIN_TILE)

            def take_y(c, h, r, i):
                act.wait_ge(y_round, r + 1)
                bank = 6 + (3 * h + i) % 2
                if i < 2:
                    a.activation(yrow[:, 4 * i:4 * i + 4, P * h:P * h + P],
                                 ps[:, bank, :].rearrange("p (b n) -> p b n", n=P), ACT.Copy).then_inc(y_round_free, 1)
                else:
                    a.activation(yrow[0:NS, PBLK, P * h:P * h + P], ps[0:NS, bank, 0:P], ACT.Copy)\
                        .then_inc(y_round_free, 1)

            def take_tile(c, h, j, last=False):
                ge(act, y_stored[h], c * 32)
                cols = bass.ds(j * P, P)

                def store(b0, b1, n):
                    act.wait_ge(y_round_free, n)
                    act.dma_start(y_p[P * b0:P * b1, cols].rearrange("(b p) n -> p b n", p=P),
                                  yrow[:, b0:b1, P * h:P * h + P]).then_inc(y_stored[h], 16)

                for i in range(3):
                    take_y(c, h, j * 3 + i, i)
                    if last and i < 2:
                        store(4 * i, 4 * i + 4, j * 3 + i + 1)
                if not last:
                    store(0, PBLK, j * 3 + 3)
                act.wait_ge(y_round_free, j * 3 + 3)
                act.dma_start(y_s[:, cols], yrow[0:NS, PBLK, P * h:P * h + P]).then_inc(y_stored[h], 16)

            def final(j):
                act.wait_ge(tile_done, j * 2 + (FIN_TILE + 1))
                ge(act, set_free[1], j + FIN_TILE // 2)
                a.activation(thirds(sg[:]), pset(0), ACT.Sigmoid).then_inc(set_free[0], 1)

            final(0)
            take_tile(0, 0, 0)
            final(1)
            with act.Fori(1, 4) as c:
                take_tile(c - 1, 1, c * 2 - 1)
                final(c * 2)
                take_tile(c, 0, c * 2)
                final(c * 2 + 1)
            take_tile(3, 1, 7, last=True)
            for h in range(2):
                act.wait_ge(y_stored[h], 32 * 4 + 16 * h)
            act.wait_ge(pool_stored, 32 * KT)


def plan_rounds():
    plan, r = [[], []], 0
    rows_end, back_end = [0] * 12, [0] * 12

    def rows(j, at):
        nonlocal r
        for i in range(3):
            here.append((at + i, "rows", j, i, r))
            r += 1
        rows_end[j] = r

    def back(j, std=None, at=4):
        nonlocal r
        for i in range(5):
            if i == 2 and std is not None:
                here.append((0, "std", std, 0, 0))
            here.append((at + i * 3 // 5, "back", j, i, r))
            r += 1
        back_end[j] = r

    for j in range(2, 13):
        here = []
        if j == 2:
            rows(0, 1)
            here.append((0, "std", 0, 0, 0))
            rows(1, 4)
        else:
            if j == 4:
                here.append((0, "std", 2, 0, 0))
            if j == 7:
                back(4, at=0)
            rows(j - 1, 2 if j == 7 else 1)
            if j == 3:
                here.append((0, "std", 1, 0, 0))
            if j < 12:
                back(j - 2 if j >= 7 else j - 3, j - 1 if 5 <= j <= 10 else None, 5 if j == 7 else 4)
            if j == 4:
                here.append((0, "std", 3, 0, 0))
        plan.append(here)
    return plan, rows_end, back_end, r


PLAN, ROWS_END, BACK_END, ROUNDS = plan_rounds()

_IN = (("x_prompt", (SEQ, D)), ("x_sample", (NS, D)), ("cache_k", (NB, P, NKV * HD)), ("cache_v", (NB, P, NKV * HD)),
       ("state_pool", (NB * HIST, D)), ("p_prompt", (SEQ, PLE)), ("p_sample", (NS, PLE)), ("params", None),
       ("w_in", (D, 6656)), ("pool_map", (4, 256, 256)), ("w_proj_pool", (D, D)), ("w_proj_attn", (D, D)),
       ("w_out", (D, D)), ("w_ple", (PLE, D)), ("w_ple_gate", (D, D)), ("const", None), ("masks", None),
       ("smask", None))
_OUT = (("y_p", (SEQ, D)), ("y_s", (NS, D)), ("nk_p", (P, 256)), ("nv_p", (P, 256)), ("npool_p", (HIST, D)),
        ("nk_s", (NB, P, 256)), ("nv_s", (NB, P, 256)), ("npool_s", (NB * HIST, D)))


def kernel(**inputs):
    import concourse.bacc as bacc
    from concourse.bass_utils import run_bass_kernel_spmd

    x = {k: np.asarray(v) for k, v in inputs.items()}
    cols = [x["norm_g"].reshape(8, P).T, x["pool_scale"].reshape(8, P).T]
    for name in ("q_norm_g", "k_norm_g", "sinks"):
        cols.append(np.broadcast_to(x[name].reshape(1, -1), (P, x[name].size)))
    cols.append(np.repeat(x["sinks"].reshape(NKV, G).T, NS, axis=0))
    x["params"] = np.concatenate(cols, axis=1)
    x["const"], x["masks"], x["smask"] = consts()
    nc = bacc.Bacc("TRN2", target_bir_lowering=False, num_devices=1)
    arrays, args = {}, []
    for name, shape in _IN:
        arr = np.ascontiguousarray(x[name] if shape is None else x[name].reshape(shape))
        arrays[f"in_{name}"] = arr
        args.append(nc.dram_tensor(f"in_{name}", arr.shape, mybir.dt.from_np(arr.dtype), kind="ExternalInput").ap())
    for name, shape in _OUT:
        args.append(nc.dram_tensor(f"out_{name}", shape, F32, kind="ExternalOutput").ap())
    build(nc, *args)
    r = run_bass_kernel_spmd(nc, [arrays], core_ids=[0]).results[0]
    o = {name: r[f"out_{name}"] for name, _ in _OUT}
    return (o["y_p"].reshape(1, SEQ, D), o["y_s"].reshape(NB, NT, D), o["nk_p"].reshape(1, 1, P, NKV, HD),
            o["nv_p"].reshape(1, 1, P, NKV, HD), o["npool_p"].reshape(1, 1, HIST, D),
            o["nk_s"].reshape(1, NB, P, NKV, HD), o["nv_s"].reshape(1, NB, P, NKV, HD),
            o["npool_s"].reshape(1, NB, HIST, D))
```
